# Optimizing a Trainium2 kernel written in Bass

```python
import math
import jax, jax.numpy as jnp
from jax import lax
import numpy as np

D_MODEL = 1024
BATCH = 1
SEQ = 256
DEPTH = 1
DEC_BATCH = 1
DEC_SEQ = 512
PAST_LEN = 128

D_MIX = D_MODEL
MLA_HEADS = 8
MLA_NOPE = 64
MLA_ROPE = 32
MLA_V = 64
Q_RANK = 256
KV_RANK = 128
DIFF_HEADS = 4
DIFF_HEAD_DIM = 64
DIFF_ROT = DIFF_HEAD_DIM // 4
ROPE_THETA = 500000.0
Q_BLOCK = 128
N_GROUPS = 4
EXPERTS_PER_GROUP = 8
N_EXPERTS = N_GROUPS * EXPERTS_PER_GROUP
TOP_K_IN_GROUP = 2
EXPERT_FF = 256
EPS = 1e-6

D_DIFF_QK = DIFF_HEADS * 2 * DIFF_HEAD_DIM
D_DIFF_V = DIFF_HEADS * 2 * DIFF_HEAD_DIM
SPLIT_POINTS = (Q_RANK, Q_RANK + KV_RANK, Q_RANK + KV_RANK + MLA_ROPE,
                Q_RANK + KV_RANK + MLA_ROPE + D_DIFF_QK,
                Q_RANK + KV_RANK + MLA_ROPE + 2 * D_DIFF_QK)
D_IN = Q_RANK + KV_RANK + MLA_ROPE + 2 * D_DIFF_QK + D_DIFF_V

kernel_name = "hybrid_mla_diffattn_hmoe_encoder"

def _rmsnorm(x, g):
    xf = x.astype(jnp.float32)
    y = xf * lax.rsqrt(jnp.mean(xf * xf, axis=-1, keepdims=True) + EPS)
    return (y * g.astype(jnp.float32)).astype(x.dtype)

def _rope(x, rot_dim):
    S = x.shape[-2]
    half = rot_dim // 2
    inv = ROPE_THETA ** (-jnp.arange(half, dtype=jnp.float32) / half)
    ang = jnp.arange(S, dtype=jnp.float32)[:, None] * inv[None, :]
    cos, sin = jnp.cos(ang), jnp.sin(ang)
    xr = x[..., :rot_dim].astype(jnp.float32)
    x1, x2 = xr[..., :half], xr[..., half:]
    rot = jnp.concatenate([x1 * cos - x2 * sin, x2 * cos + x1 * sin], axis=-1).astype(x.dtype)
    return jnp.concatenate([rot, x[..., rot_dim:]], axis=-1)

def _blocked_attention(q, k, v, scale):
    B, H, S, dk = q.shape
    dv = v.shape[-1]
    nb = S // Q_BLOCK
    qb = q.reshape(B, H, nb, Q_BLOCK, dk).transpose(2, 0, 1, 3, 4)

    def one(qi):
        s = jnp.einsum('bhqd,bhkd->bhqk', qi, k).astype(jnp.float32) * scale
        p = jax.nn.softmax(s, axis=-1)
        return jnp.einsum('bhqk,bhkd->bhqd', p.astype(v.dtype), v)

    o = lax.map(one, qb)
    return o.transpose(1, 2, 0, 3, 4).reshape(B, H, S, dv)

def _blocked_diff_attention(q, k, v, lam, scale):
    B, H, _, S, d = q.shape
    dv = v.shape[-1]
    nb = S // Q_BLOCK
    qb = q.reshape(B, H, 2, nb, Q_BLOCK, d).transpose(3, 0, 1, 2, 4, 5)

    def one(qi):
        s = jnp.einsum('bhcqd,bhckd->bhcqk', qi, k).astype(jnp.float32) * scale
        p = jax.nn.softmax(s, axis=-1)
        a = p[:, :, 0] - lam * p[:, :, 1]
        return jnp.einsum('bhqk,bhkd->bhqd', a.astype(v.dtype), v)

    o = lax.map(one, qb)
    return o.transpose(1, 2, 0, 3, 4).reshape(B, H, S, dv)

def _mla(c_q, c_kv, k_pe, q_norm, w_uq, kv_norm, w_ukv):
    B, S, _ = c_q.shape
    q = (_rmsnorm(c_q, q_norm) @ w_uq).reshape(B, S, MLA_HEADS, MLA_NOPE + MLA_ROPE).transpose(0, 2, 1, 3)
    q = jnp.concatenate([q[..., :MLA_NOPE], _rope(q[..., MLA_NOPE:], MLA_ROPE)], axis=-1)
    kv = (_rmsnorm(c_kv, kv_norm) @ w_ukv).reshape(B, S, MLA_HEADS, MLA_NOPE + MLA_V).transpose(0, 2, 1, 3)
    k_nope, v = kv[..., :MLA_NOPE], kv[..., MLA_NOPE:]
    k_rot = _rope(k_pe[:, None], MLA_ROPE)
    k = jnp.concatenate([k_nope, jnp.broadcast_to(k_rot, (B, MLA_HEADS, S, MLA_ROPE))], axis=-1)
    o = _blocked_attention(q, k, v, (MLA_NOPE + MLA_ROPE) ** -0.5)
    return o.transpose(0, 2, 1, 3).reshape(B, S, MLA_HEADS * MLA_V)

def _diff_attention(dq, dk, dv, lq1, lk1, lq2, lk2, subln, lambda_init):
    B, S, _ = dq.shape
    q = _rope(dq.reshape(B, S, DIFF_HEADS, 2, DIFF_HEAD_DIM).transpose(0, 2, 3, 1, 4), DIFF_ROT)
    k = _rope(dk.reshape(B, S, DIFF_HEADS, 2, DIFF_HEAD_DIM).transpose(0, 2, 3, 1, 4), DIFF_ROT)
    v = dv.reshape(B, S, DIFF_HEADS, 2 * DIFF_HEAD_DIM).transpose(0, 2, 1, 3)
    lam = (jnp.exp(jnp.sum(lq1.astype(jnp.float32) * lk1.astype(jnp.float32)))
           - jnp.exp(jnp.sum(lq2.astype(jnp.float32) * lk2.astype(jnp.float32))) + lambda_init)
    o = _blocked_diff_attention(q, k, v, lam, DIFF_HEAD_DIM ** -0.5)
    o = _rmsnorm(o, subln) * (1.0 - lambda_init)
    return o.transpose(0, 2, 1, 3).reshape(B, S, DIFF_HEADS * 2 * DIFF_HEAD_DIM)

def _hier_moe(h, router_group, router_group_bias, router_expert, router_expert_bias, w_gate, w_up, w_down):
    B, S, D = h.shape
    t = h.reshape(B * S, D)
    gl = (t @ router_group).astype(jnp.float32) + router_group_bias.astype(jnp.float32)
    gp = jax.nn.softmax(gl, axis=-1)
    p_g, g_idx = lax.top_k(gp, 1)
    el = ((t @ router_expert).astype(jnp.float32)
          + router_expert_bias.astype(jnp.float32)).reshape(-1, N_GROUPS, EXPERTS_PER_GROUP)
    within = jnp.einsum('tg,tge->te', jax.nn.one_hot(g_idx[:, 0], N_GROUPS, dtype=jnp.float32), el)
    wp = jax.nn.softmax(within, axis=-1)
    w2, e2 = lax.top_k(wp, TOP_K_IN_GROUP)
    w2 = w2 / jnp.sum(w2, axis=-1, keepdims=True)
    e_global = g_idx * EXPERTS_PER_GROUP + e2
    gates = jnp.einsum('tk,tke->te', p_g * w2,
                       jax.nn.one_hot(e_global, N_EXPERTS, dtype=jnp.float32)).astype(t.dtype)
    out = jnp.zeros_like(t)
    for e in range(N_EXPERTS):
        y = (jax.nn.silu(t @ w_gate[e]) * (t @ w_up[e])) @ w_down[e]
        out = out + gates[:, e:e + 1] * y
    return out.reshape(B, S, D)

def _forward(x, attn_norm, w_in, q_norm, w_uq, kv_norm, w_ukv, diff_lq1, diff_lk1, diff_lq2, diff_lk2,
             diff_subln, w_out, ffn_norm, router_group, router_group_bias, router_expert,
             router_expert_bias, w_gate, w_up, w_down, final_norm):
    for l in range(DEPTH):
        lambda_init = 0.8 - 0.6 * math.exp(-0.3 * l)
        h = _rmsnorm(x, attn_norm[l])
        proj = h @ w_in[l]
        c_q, c_kv, k_pe, dq, dk, dv = jnp.split(proj, SPLIT_POINTS, axis=-1)
        a = _mla(c_q, c_kv, k_pe, q_norm[l], w_uq[l], kv_norm[l], w_ukv[l])
        b = _diff_attention(dq, dk, dv, diff_lq1[l], diff_lk1[l], diff_lq2[l], diff_lk2[l],
                            diff_subln[l], lambda_init)
        x = x + jnp.concatenate([a, b], axis=-1) @ w_out[l]
        x = x + _hier_moe(_rmsnorm(x, ffn_norm[l]), router_group[l], router_group_bias[l],
                          router_expert[l], router_expert_bias[l], w_gate[l], w_up[l], w_down[l])
    return _rmsnorm(x, final_norm)

def setup_inputs(seed: int = 0) -> dict:
    key = jax.random.key(seed)
    ks = jax.random.split(key, 24)
    L = DEPTH

    def w(k, shape, fan_in):
        return jax.random.normal(k, shape, jnp.float32) * (fan_in ** -0.5)

    def gain(k, shape):
        return 1.0 + 0.02 * jax.random.normal(k, shape, jnp.float32)

    return {
        "x_prompt": jax.random.normal(ks[0], (BATCH, SEQ, D_MODEL), jnp.float32),
        "x_sample": jax.random.normal(ks[1], (DEC_BATCH, DEC_SEQ, D_MODEL), jnp.float32),
        "attn_norm": gain(ks[2], (L, D_MODEL)),
        "w_in": w(ks[3], (L, D_MODEL, D_IN), D_MODEL),
        "q_norm": gain(ks[4], (L, Q_RANK)),
        "w_uq": w(ks[5], (L, Q_RANK, MLA_HEADS * (MLA_NOPE + MLA_ROPE)), Q_RANK),
        "kv_norm": gain(ks[6], (L, KV_RANK)),
        "w_ukv": w(ks[7], (L, KV_RANK, MLA_HEADS * (MLA_NOPE + MLA_V)), KV_RANK),
        "diff_lq1": 0.1 * jax.random.normal(ks[8], (L, DIFF_HEAD_DIM), jnp.float32),
        "diff_lk1": 0.1 * jax.random.normal(ks[9], (L, DIFF_HEAD_DIM), jnp.float32),
        "diff_lq2": 0.1 * jax.random.normal(ks[10], (L, DIFF_HEAD_DIM), jnp.float32),
        "diff_lk2": 0.1 * jax.random.normal(ks[11], (L, DIFF_HEAD_DIM), jnp.float32),
        "diff_subln": gain(ks[12], (L, 2 * DIFF_HEAD_DIM)),
        "w_out": w(ks[13], (L, D_MIX, D_MODEL), D_MIX),
        "ffn_norm": gain(ks[14], (L, D_MODEL)),
        "router_group": w(ks[15], (L, D_MODEL, N_GROUPS), D_MODEL),
        "router_group_bias": 0.01 * jax.random.normal(ks[16], (L, N_GROUPS), jnp.float32),
        "router_expert": w(ks[17], (L, D_MODEL, N_EXPERTS), D_MODEL),
        "router_expert_bias": 0.01 * jax.random.normal(ks[18], (L, N_EXPERTS), jnp.float32),
        "w_gate": w(ks[19], (L, N_EXPERTS, D_MODEL, EXPERT_FF), D_MODEL),
        "w_up": w(ks[20], (L, N_EXPERTS, D_MODEL, EXPERT_FF), D_MODEL),
        "w_down": w(ks[21], (L, N_EXPERTS, EXPERT_FF, D_MODEL), EXPERT_FF),
        "final_norm": gain(ks[22], (D_MODEL,)),
    }

def reference(x_prompt, x_sample, attn_norm, w_in, q_norm, w_uq, kv_norm, w_ukv, diff_lq1, diff_lk1,
              diff_lq2, diff_lk2, diff_subln, w_out, ffn_norm, router_group, router_group_bias,
              router_expert, router_expert_bias, w_gate, w_up, w_down, final_norm):
    y_prompt = _forward(x_prompt, attn_norm, w_in, q_norm, w_uq, kv_norm, w_ukv, diff_lq1, diff_lk1,
                        diff_lq2, diff_lk2, diff_subln, w_out, ffn_norm, router_group, router_group_bias,
                        router_expert, router_expert_bias, w_gate, w_up, w_down, final_norm)
    y_sample = _forward(x_sample, attn_norm, w_in, q_norm, w_uq, kv_norm, w_ukv, diff_lq1, diff_lk1,
                        diff_lq2, diff_lk2, diff_subln, w_out, ffn_norm, router_group, router_group_bias,
                        router_expert, router_expert_bias, w_gate, w_up, w_down, final_norm)
    return (y_prompt, y_sample)


_drawn_inputs = setup_inputs


def setup_inputs(seed=0):
    import zlib

    import numpy as np

    out = dict(_drawn_inputs(seed))
    spreads = {}
    factors = {'q_norm': 4.303,
     'kv_norm': 5.174,
     'diff_lk1': 39.951,
     'diff_lq2': 38.404,
     'router_group_bias': 38.384,
     'router_expert_bias': 16.583,
     'final_norm': 7.959,
     'diff_subln': 8.0,
     'ffn_norm': 6.256}
    for name, (base, spread) in spreads.items():
        noise = np.random.default_rng([zlib.crc32(name.encode()), seed]).standard_normal(out[name].shape)
        drawn = base * np.exp(spread * noise) if base else spread * noise
        out[name] = __import__('jax').numpy.asarray(drawn.astype(out[name].dtype))
    for name, factor in factors.items():
        out[name] = (out[name] * factor).astype(out[name].dtype)
    return out
```

```python
import math
from contextlib import ExitStack

import numpy as np
import concourse.bass as bass
from concourse import mybir

P = 128
D = 1024
S_PROMPT, S_SAMPLE = 256, 512
T = S_PROMPT + S_SAMPLE
NT = T // P
DC = D // P
Q_RANK, KV_RANK, ROPE = 256, 128, 32
HEADS, NOPE, VD = 8, 64, 64
QK = NOPE + ROPE
DH, DD = 4, 64
ROT = DD // 4
LATENT = Q_RANK + KV_RANK + ROPE
GROUP_COLS = [LATENT, DH * 2 * DD, DH * 2 * DD, DH * 2 * DD]
GROUP_AT = [0, LATENT, LATENT + 512, LATENT + 1024]
NG, EPG = 4, 8
NE = NG * EPG
FF = 256
EPS = 1e-6
THETA = 500000.0
LAMBDA_INIT = 0.8 - 0.6 * math.exp(-0.3 * 0)
MLA_SCALE = QK ** -0.5
DIFF_SCALE = DD ** -0.5
SLOTS = 64
NBLK = T // SLOTS
RING = 4
SLOT_W = 3 * D * FF // P
MAGIC = 0x5F3759DF

CONST = {}
_at = 0
for _n, _w in (("ident", P), ("upper", P), ("cos_m", 4 * 16), ("sin_m", 4 * 16), ("cos_d", 4 * 8),
               ("sin_d", 4 * 8), ("iota_e", NE), ("rev_e", NE), ("rev_g", NG), ("steps", NBLK - 1),
               ("pack4", RING), ("before_g", 64), ("map_rows", 2)):
    CONST[_n] = (_at, _w)
    _at += _w
CONST_W = _at


def constants():
    c = np.zeros((P, CONST_W), np.float32)

    def put(name, value):
        a, w = CONST[name]
        c[:, a:a + w] = np.asarray(value, np.float32).reshape(-1, w)

    put("ident", np.eye(P))
    put("upper", np.triu(np.ones((P, P)), 1))
    for rot, cn, sn in ((ROPE, "cos_m", "sin_m"), (ROT, "cos_d", "sin_d")):
        half = rot // 2
        inv = np.float32(THETA) ** (-np.arange(half, dtype=np.float32) / np.float32(half))
        ang = np.arange(S_SAMPLE, dtype=np.float32)[:, None] * inv.astype(np.float32)[None, :]
        put(cn, np.cos(ang).reshape(4, P, half).transpose(1, 0, 2))
        put(sn, np.sin(ang).reshape(4, P, half).transpose(1, 0, 2))
    put("iota_e", np.arange(NE))
    put("rev_e", NE - np.arange(NE))
    put("rev_g", NG - np.arange(NG))
    put("steps", SLOTS * np.arange(1, NBLK))
    put("pack4", 16.0 ** np.arange(RING))
    put("map_rows", np.arange(P)[:, None] // DD == np.arange(2)[None, :])
    g = np.arange(8)
    put("before_g", 65536.0 * (g[None, :] < g[:, None]))
    return c


def units():
    out = []
    for seq0, nt in ((0, 2), (2, 4)):
        for j in range(4):
            for qt in range(nt):
                out += [(seq0, nt, "mla", j, qt), (seq0, nt, "diff", j, qt)]
    return out


UNITS = units()
N_UNITS = len(UNITS)
BEFORE = [sum(1 for v in UNITS[:u] if v[2] == UNITS[u][2]) for u in range(N_UNITS)]


def is_mla(u):
    return UNITS[u][2] == "mla"


def batch(u):
    seq0, nt, kind, j, qt = UNITS[u]
    return j + (4 if seq0 else 0)


def ends_batch(u):
    return not is_mla(u) and UNITS[u][4] == UNITS[u][1] - 1


TRANSPOSES = []
for _i in range(N_UNITS + 6):
    if 0 <= _i - 2 < N_UNITS:
        TRANSPOSES += [("p", _i - 2, a) for a in range(2 if is_mla(_i - 2) else 1)]
    if 0 <= _i - 5 < N_UNITS and ends_batch(_i - 5):
        TRANSPOSES.append(("o", _i - 5, 0))
TURN = {x: n for n, x in enumerate(TRANSPOSES)}


def p_transposed(u):
    return TURN[("p", u, 1 if is_mla(u) else 0)] + 1


def build(nc, A):
    f32, u32, i32, bf16 = (mybir.dt.float32, mybir.dt.uint32, mybir.dt.int32, mybir.dt.bfloat16)
    ALU = mybir.AluOpType
    ACT = mybir.ActivationFunctionType
    X_ = mybir.AxisListType.X

    h2_dram = nc.dram_tensor("h2_rows", (T, D), f32).ap()
    ids_dram = nc.dram_tensor("pair_of_slot", (T * NE, 1), u32).ap()
    y_dram = nc.dram_tensor("pair_rows", (4 * T, D // 2), f32).ap()

    with ExitStack() as ctx:
        def sem(name):
            return ctx.enter_context(nc.semaphore(name))

        WORDS = 53200
        arena = ctx.enter_context(nc.sbuf_tensor("arena", [P, WORDS], f32))
        psum = ctx.enter_context(nc.psum_tensor("banks", [P, 8, 512], f32))

        def bank(b):
            return psum[:, b, :]

        class Area:

            def __init__(self, at, end):
                self.at, self.end = at, end

            def take(self, words):
                a = self.at
                self.at += words
                assert self.at <= self.end, (self.at, self.end)
                return arena[:, a:a + words]

        X0 = 0
        W0 = X0 + NT * D
        QKV0 = W0 + 2 * DC * 512
        R0 = QKV0 + RING * SLOT_W
        K0 = R0 + DC * T
        M0 = K0 + 1216

        x_tok = arena[:, X0:X0 + NT * D].rearrange("p (t d) -> p t d", t=NT)
        xgT = arena[:, R0:R0 + DC * T].rearrange("p (t c n) -> p t c n", t=NT, c=DC)
        aT = arena[:, R0:R0 + DC * T].rearrange("p (c n) -> p c n", c=DC)
        w_buf = [arena[:, W0 + i * 4096:W0 + (i + 1) * 4096] for i in range(2)]
        w_out_sb = arena[:, W0:W0 + 8192].rearrange("p (c n) -> p c n", c=DC)
        q = Area(QKV0, R0)
        qT = q.take(HEADS * T).rearrange("p (h n) -> p h n", h=HEADS)
        kT = q.take(HEADS * T).rearrange("p (h n) -> p h n", h=HEADS)
        v_tok = q.take(NT * 512).rearrange("p (t n) -> p t n", t=NT)
        vd_words = q.take(NT * 512)
        vd_tok = vd_words.rearrange("p (t n) -> p t n", t=NT)
        w_uq_sb = vd_words[:, 0:2 * 768].rearrange("p (c n) -> p c n", c=2)
        w_ukv_sb = vd_words[:, 1536:1536 + 1024]
        qdT = q.take(DH * T).rearrange("p (h n) -> p h n", h=DH)
        kdT = q.take(DH * T).rearrange("p (h n) -> p h n", h=DH)
        ring = [arena[:, QKV0 + s * SLOT_W:QKV0 + (s + 1) * SLOT_W] for s in range(RING)]

        k = Area(K0, M0)
        const_sb = k.take(CONST_W)

        def const(name):
            a, w = CONST[name]
            return const_sb[:, a:a + w]

        ident = const("ident")
        gain_in = k.take(DC)
        gains = k.take(4)
        gain_q, gain_kv, gain_sub = gains[:, 0:2], gains[:, 2:3], gains[:, 3:4]
        pairid = k.take(2 * NT).bitcast(u32)
        slot_u = k.take(2 * NT).bitcast(u32)
        gates = k.take(2 * NT)
        ids_sb = k.take(NBLK * NE).bitcast(u32)
        neglam = k.take(1)
        ss = k.take(NT)
        rs = k.take(NT)
        ss_c = k.take(2 * NT)
        rs_c = k.take(2 * NT)
        nw = k.take(3 * 8)

        m = Area(M0, WORDS)
        c_tok = [m.take(LATENT) for _ in range(3)]
        qk_tok = [m.take(512) for _ in range(2)]
        q_tok = m.take(HEADS * QK)
        k_tok = m.take(HEADS * QK)
        cT = [m.take(3 * P) for _ in range(2)]
        rope_t = m.take(4 * P)
        kpe_t = m.take(4 * 16 + ROPE)
        junk = m.take(512).bitcast(bf16)
        junk_l = m.take(192).bitcast(bf16)
        lam_in = m.take(4 * DD)
        lam_t = m.take(DD)
        lam_s = m.take(4)
        m = Area(M0, WORDS)
        p_tok = [m.take(1024).rearrange("p (a n) -> p a n", a=2) for _ in range(3)]
        pT = [m.take(1024).rearrange("p (a k n) -> p a k n", a=2, k=4) for _ in range(2)]
        q_pad = [m.take(2 * P).rearrange("p (a n) -> p a n", a=2) for _ in range(2)]
        od = [m.take(512).rearrange("p (q n) -> p q n", q=4) for _ in range(2)]
        mx = m.take(8).rearrange("p (u a) -> p u a", a=2)
        nbias = m.take(8).rearrange("p (u a) -> p u a", a=2)
        l_sum = m.take(12).rearrange("p (u a) -> p u a", a=2)
        rl = m.take(12).rearrange("p (u a) -> p u a", a=2)
        cmix = m.take(2)
        so = m.take(8)
        ro = m.take(8)
        junk_o = m.take(64).bitcast(bf16)
        m = Area(M0, WORDS)
        h2 = [m.take(D) for _ in range(2)]
        h2T = m.take(D).rearrange("p (c n) -> p c n", c=DC)
        gain_ffn = m.take(D)
        m1_all = m.take(NT * NE).rearrange("p (t e) -> p t e", t=NT)
        m2_all = m.take(NT * NE).rearrange("p (t e) -> p t e", t=NT)
        m12 = m.take(NT * NE).rearrange("p (t e) -> p t e", t=NT)
        macc = m.take(NT * NE).rearrange("p (t e) -> p t e", t=NT)
        w_r = m.take(DC * (NG + NE)).rearrange("p (c n) -> p c n", c=DC)
        bias_r = m.take(NG + NE)
        ones = m.take(P)
        logit = m.take(NG + NE)
        r_small = m.take(16)
        r_g = m.take(3 * NG)
        r_e = m.take(4 * NE)
        slot_f = m.take(2)
        junk_c = m.take(512).bitcast(bf16)
        cnt = m.take(NE)
        over = m.take(NE * (NBLK - 1))
        extra = m.take(NE)
        pk = m.take(64)
        packed_i = k.take(8).bitcast(i32)
        yids_sb = m.take(NBLK * NE).bitcast(u32)
        m = Area(W0, QKV0)
        x_rows = [m.take(D) for _ in range(RING + 1)]
        x_eT = [m.take(DC * SLOTS).rearrange("p (c n) -> p c n", c=DC) for _ in range(3)]
        silu_t = [m.take(P) for _ in range(3)]
        h_tok = [m.take(P) for _ in range(3)]
        h_T = [m.take(P) for _ in range(2)]
        id_cur = m.take(RING + 1).bitcast(u32)
        yid_cur = m.take(3).bitcast(u32)
        gain_fin = arena[:, M0:M0 + D]
        y_rows = arena[:, QKV0:QKV0 + 2 * NT * D].rearrange("p (i d) -> p i d", i=2 * NT)
        junk_e = arena[:, M0 + D:M0 + D + 512].bitcast(bf16)
        y_sb = [arena[:, M0 + D + 512 * i:M0 + D + 512 * (i + 1)] for i in range(1, 4)]

        x_in = [sem(f"x_in{t}") for t in range(NT)]
        xT_in = [sem(f"xT_in{t}") for t in range(NT)]
        win_in = [sem(f"win_in{g}") for g in range(4)]
        const_in = sem("const_in")
        gain_loaded = sem("gain_loaded")
        wup_in = sem("wup_in")
        lam_loaded = sem("lam_loaded")
        wout_in = sem("wout_in")
        router_in = sem("router_in")
        gffn_in = sem("gffn_in")
        gfin_in = sem("gfin_in")
        dve_chain = sem("dve_chain")
        act_chain = sem("act_chain")
        pool_chain = sem("pool_chain")
        xg_ready = sem("xg_ready")
        ss_ready = sem("ss_ready")
        rs_ready = sem("rs_ready")
        proj_done = sem("proj_done")
        proj_out = sem("proj_out")
        ssc_ready = sem("ssc_ready")
        rsc_ready = sem("rsc_ready")
        cT_psum = sem("cT_psum")
        cT_ready = sem("cT_ready")
        up_done = sem("up_done")
        q_out = sem("q_out")
        kv_out = sem("kv_out")
        q_roped = sem("q_roped")
        k_roped = sem("k_roped")
        qkT_psum = sem("qkT_psum")
        qT_ready = sem("qT_ready")
        kT_ready = sem("kT_ready")
        d_roped = sem("d_roped")
        dT_psum = sem("dT_psum")
        dT_ready = sem("dT_ready")
        zero_ready = sem("zero_ready")
        ones_ready = sem("ones_ready")
        lam_e = sem("lam_e")
        lam_ready = sem("lam_ready")

        scores = sem("scores")
        nbias_ready = sem("nbias_ready")
        exps = sem("exps")
        qpad_ready = sem("qpad_ready")
        rl_ready = sem("rl_ready")
        p_normed = sem("p_normed")
        p_mixed = sem("p_mixed")
        pT_psum = sem("pT_psum")
        pT_dve = sem("pT_dve")
        pT_act = sem("pT_act")
        pv_done = sem("pv_done")
        o_mla = sem("o_mla")
        o_diff = sem("o_diff")
        ro_ready = sem("ro_ready")
        od_scaled = sem("od_scaled")
        odT_ready = sem("odT_ready")

        oproj = sem("oproj")
        x2_ready = sem("x2_ready")
        ss2_ready = sem("ss2_ready")
        h2_ready = sem("h2_ready")
        h2_stored = [sem(f"h2_stored{i}") for i in range(2)]
        h2T_psum = sem("h2T_psum")
        h2T_ready = sem("h2T_ready")
        logits = sem("logits")
        route_neg = sem("route_neg")
        route_exp = sem("route_exp")
        masks = sem("masks")
        ranks = sem("ranks")
        slots_ready = sem("slots_ready")
        counts_psum = sem("counts_psum")
        counts_ready = sem("counts_ready")
        ids_zeroed = sem("ids_zeroed")
        ids_scattered = sem("ids_scattered")
        ids_loaded = sem("ids_loaded")
        ids_ready = sem("ids_ready")
        yid_ready = sem("yid_ready")
        pool_waited = sem("pool_waited")
        pe_waited = sem("pe_waited")
        e_yid = sem("e_yid")

        w_loaded = [sem(f"w_loaded{s}") for s in range(RING)]
        id_ready = sem("id_ready")
        rows_in = [sem(f"rows_in{i}") for i in range(RING + 1)]
        xeT_psum = sem("xeT_psum")
        xeT_ready = sem("xeT_ready")
        gu_done = sem("gu_done")
        silu_done = sem("silu_done")
        h_ready = sem("h_ready")
        hT_psum = sem("hT_psum")
        hT_ready = sem("hT_ready")
        down_done = sem("down_done")
        y_out = sem("y_out")
        y_stored = [sem(f"y_stored{i}") for i in range(3)]
        e_id = sem("e_id")
        e_xeT_psum = sem("e_xeT_psum")
        e_xeT = sem("e_xeT")
        e_gu = sem("e_gu")
        e_silu = sem("e_silu")
        e_h = sem("e_h")
        e_hT_psum = sem("e_hT_psum")
        e_hT = sem("e_hT")
        e_down = sem("e_down")
        e_y = sem("e_y")
        all_stored = sem("all_stored")
        yrows_in = [sem(f"yrows_in{t}") for t in range(NT)]
        y_added = sem("y_added")
        ss3_ready = sem("ss3_ready")
        final_ready = sem("final_ready")
        out_stored = sem("out_stored")

        block = ctx.enter_context(nc.Block())

        win_v = A["w_in"].rearrange("(p c) n -> p c n", c=DC)

        def group_w(g):
            return w_buf[g % 2][:, 0:DC * GROUP_COLS[g]].rearrange("p (c n) -> p c n", c=DC)

        def extras(v, s):
            n = nc.s_assert_within((v // 16 ** s) % 16, 0, NBLK - 1, skip_runtime_bounds_check_because=(
                "an expert has at most T tokens"))
            before = v // 65536
            for i in range(s):
                before = before + (v // 16 ** i) % 16
            return n, before

        @block.sync
        def _(sp):
            sp.dma_start(gain_in, A["attn_norm"].rearrange("o (p c) -> (o p) c", c=DC)).then_inc(gain_loaded, 16)
            sp.dma_start(xgT[:, 0, :, :], A["xT"][:, 0, :, :]).then_inc(xT_in[0], 16)
            sp.dma_start(group_w(0), win_v[:, :, 0:LATENT]).then_inc(win_in[0], 16)
            sp.dma_start(x_tok[:, 0, :], A["x"][0:P, :]).then_inc(x_in[0], 16)
            sp.dma_start(const_sb, A["consts"]).then_inc(const_in, 16)
            sp.dma_start(gains, A["gains"]).then_inc(const_in, 16)
            sp.dma_start(pairid, A["pairid"]).then_inc(const_in, 16)
            for t in range(1, NT):
                sp.dma_start(xgT[:, t, :, :], A["xT"][:, t, :, :]).then_inc(xT_in[t], 16)
                sp.dma_start(x_tok[:, t, :], A["x"][t * P:(t + 1) * P, :]).then_inc(x_in[t], 16)
                if t == 1:
                    sp.dma_start(w_uq_sb, A["w_uq"][0].rearrange("(c p) n -> p c n", p=P)).then_inc(wup_in, 16)
                    sp.dma_start(w_ukv_sb, A["w_ukv"][0]).then_inc(wup_in, 16)
                    for i, n in enumerate(("diff_lq1", "diff_lk1", "diff_lq2", "diff_lk2")):
                        sp.dma_start(lam_in[:, i * DD:(i + 1) * DD],
                                     A[n].to_broadcast([P, DD])).then_inc(lam_loaded, 16)
            for g in range(1, 4):
                if g >= 2:
                    sp.wait_ge(proj_done, 6 * (g - 2) + 6)
                sp.dma_start(group_w(g), win_v[:, :, GROUP_AT[g]:GROUP_AT[g] + 512]).then_inc(win_in[g], 16)
            sp.wait_ge(proj_done, 24)
            sp.dma_start(w_out_sb, A["w_out"][0].rearrange("(c p) n -> p c n", p=P)).then_inc(wout_in, 16)
            sp.wait_ge(zero_ready, 1)
            sp.dma_start(ids_dram.rearrange("(b r e) o -> r b (e o)", b=NBLK, e=NE),
                         ids_sb[0:SLOTS, :].rearrange("r (b e) -> r b e", b=NBLK)).then_inc(ids_zeroed, 16)
            sp.wait_ge(odT_ready, 8)
            sp.wait_ge(o_mla, N_UNITS // 2)
            sp.dma_start(gain_ffn, A["ffn_norm"].to_broadcast([P, D])).then_inc(gffn_in, 16)
            sp.dma_start(w_r[:, :, 0:NG], A["router_group"][0].rearrange("(p c) n -> p c n", c=DC)).then_inc(router_in, 16)
            sp.dma_start(w_r[:, :, NG:NG + NE], A["router_expert"][0].rearrange("(p c) n -> p c n", c=DC)).then_inc(router_in, 16)
            sp.dma_start(bias_r[:, 0:NG], A["router_group_bias"].to_broadcast([P, NG])).then_inc(router_in, 16)
            sp.dma_start(bias_r[:, NG:NG + NE], A["router_expert_bias"].to_broadcast([P, NE])).then_inc(router_in, 16)

            def load_expert(g, s):
                e = g * RING + s
                if not isinstance(g, int) or g > 0:
                    sp.wait_ge(down_done, e - RING + 1)
                for i, n in enumerate(("w_gate", "w_up")):
                    sp.dma_start(ring[s][:, i * 2048:(i + 1) * 2048],
                                 A[n][0, bass.ds(e, 1), :, :].rearrange("o (p c) n -> p (o c n)", c=DC)
                                 ).then_inc(w_loaded[s], 16)
                sp.dma_start(ring[s][:, 4096:6144].rearrange("p (j n) -> p j n", j=2),
                             A["w_down"][0, bass.ds(e, 1), :, :].rearrange("o (j p) n -> p (o j) n", p=P)
                             ).then_inc(w_loaded[s], 16)

            sp.wait_ge(pv_done, N_UNITS)
            for s in range(RING):
                load_expert(0, s)
            with sp.Fori(1, NE // RING) as g:
                for s in range(RING):
                    load_expert(g, s)
            sp.wait_ge(counts_ready, 1)
            sp.wait_ge(ids_scattered, 2 * NT * 16)
            sp.wait_ge(h2_stored[0], 3 * 16)
            sp.wait_ge(h2_stored[1], 3 * 16)
            sp.dma_start(gain_fin, A["final_norm"].rearrange("(o n) -> o n", o=1).to_broadcast([P, D])).then_inc(gfin_in, 16)
            sp.wait_ge(down_done, NE)
            sp.wait_ge(all_stored, 1)
            pairs = y_dram.rearrange("(t p i) n -> t p (i n)", t=NT, i=4)
            for t in range(NT):
                sp.dma_start(y_rows[:, 2 * t:2 * t + 2, :].rearrange("p i n -> p (i n)"), pairs[t]).then_inc(yrows_in[t], 16)
            for t in range(NT):
                sp.wait_ge(final_ready, t + 1)
                out = A["y_prompt"][0, t * P:(t + 1) * P, :] if t < 2 else A["y_sample"][0, (t - 2) * P:(t - 1) * P, :]
                sp.dma_start(out, y_rows[:, 2 * t, :]).then_inc(out_stored, 16)
            sp.wait_ge(out_stored, NT * 16)

        @block.gpsimd
        def _(pool):
            chain = [0]

            def link(ins):
                chain[0] += 1
                ins.then_inc(pool_chain, 1)
                pool.wait_ge(pool_chain, chain[0])

            def rotary(x1, x2, cos, sin, t, shape):
                a = [t[:, i, 0:shape[1] * shape[2]].rearrange("p (a b) -> p a b", a=shape[1]) for i in range(4)]
                c, s = cos.to_broadcast(shape), sin.to_broadcast(shape)
                pool.tensor_tensor(a[0], x1, c, ALU.mult).then_inc(pool_chain, 1)
                pool.tensor_tensor(a[1], x2, s, ALU.mult).then_inc(pool_chain, 1)
                pool.tensor_tensor(a[2], x2, c, ALU.mult).then_inc(pool_chain, 1)
                pool.tensor_tensor(a[3], x1, s, ALU.mult).then_inc(pool_chain, 1)
                chain[0] += 4
                pool.wait_ge(pool_chain, chain[0])
                link(pool.tensor_tensor(x1, a[0], a[1], ALU.subtract))
                return pool.tensor_tensor(x2, a[2], a[3], ALU.add)

            def angle(name, t, half):
                tt = t if t < 2 else t - 2
                return const(name)[:, tt * half:(tt + 1) * half].unsqueeze(1)

            pool.memset(ids_sb, 2 * T).then_inc(zero_ready, 1)
            pool.wait_ge(const_in, 3 * 16)
            rt = rope_t.rearrange("p (i n) -> p i n", i=4)
            kt = kpe_t[:, 0:64].rearrange("p (i n) -> p i n", i=4)
            kr = kpe_t[:, 64:64 + ROPE]
            q3 = q_tok.rearrange("p (h n) -> p h n", h=HEADS)
            k3 = k_tok.rearrange("p (h n) -> p h n", h=HEADS)

            def up_rotary(t):
                pool.wait_ge(q_out, t + 1)
                last = rotary(q3[:, :, NOPE:NOPE + 16], q3[:, :, NOPE + 16:QK], angle("cos_m", t, 16),
                              angle("sin_m", t, 16), rt, [P, HEADS, 16])
                last.then_inc(q_roped, 1)
                pool.wait_ge(q_roped, t + 1)
                x = c_tok[t % 3][:, Q_RANK + KV_RANK:LATENT].unsqueeze(1)
                last = rotary(x[:, :, 0:16], x[:, :, 16:32], angle("cos_m", t, 16), angle("sin_m", t, 16),
                              kt, [P, 1, 16])
                link(last)
                if t:
                    pool.wait_ge(qkT_psum, t)
                pool.tensor_copy(k3[:, :, NOPE:QK], x.to_broadcast([P, HEADS, ROPE])).then_inc(k_roped, 1)

            for i in range(25):
                mm = i - 1
                if 6 <= mm < 18:
                    d, t = mm - 6, mm % 6
                    pool.wait_ge(proj_out, mm + 1)
                    v = qk_tok[mm % 2].rearrange("p (h n) -> p h n", h=2 * DH)
                    last = rotary(v[:, :, 0:8], v[:, :, 8:16], angle("cos_d", t, 8), angle("sin_d", t, 8),
                                  rt, [P, 2 * DH, 8])
                    last.then_inc(d_roped, 1)
                    pool.wait_ge(d_roped, d + 1)
                if 2 <= i < 8:
                    up_rotary(i - 2)

            pool.wait_ge(dT_ready, 12)
            pool.wait_ge(qT_ready, 6)
            pool.wait_ge(lam_ready, 1)
            pool.wait_ge(proj_out, 24)
            def pad(u):
                seq0, nt, kind, j, qt = UNITS[u]
                d = BEFORE[u]
                if d >= 2:
                    pool.wait_ge(scores, 2 * (u - 4) + 2)
                tok = slice((seq0 + qt) * P, (seq0 + qt + 1) * P)
                for a in range(2):
                    pool.tensor_scalar(q_pad[d % 2][:, a, :], qdT[:, j, tok], const("map_rows")[:, a:a + 1], None,
                                       ALU.mult).then_inc(qpad_ready, 1)

            pad(1)
            for u in range(N_UNITS):
                if u + 2 < N_UNITS and not is_mla(u + 2):
                    pad(u + 2)
                if is_mla(u):
                    pool.wait_ge(rl_ready, u + 1)
                    for a in range(2):
                        p = p_tok[u % 3][:, a, 0:UNITS[u][1] * P]
                        pool.tensor_scalar(p, p, rl[:, u % 6, a:a + 1], None, ALU.mult).then_inc(p_normed, 1)

            for t in range(NT):
                pool.wait_ge(h2_ready, t + 1)
                pool.dma_start(h2_dram[t * P:(t + 1) * P, :], h2[t % 2]).then_inc(h2_stored[t % 2], 16)
            pool.wait_ge(ids_zeroed, 16)
            for t in range(NT):
                pool.wait_ge(slots_ready, t + 1)
                for i in range(2):
                    pool.indirect_dma_start(ids_dram, bass.IndirectOffsetOnAxis(ap=slot_u[:, 2 * t + i:2 * t + i + 1], axis=0),
                                            pairid[:, 2 * t + i:2 * t + i + 1], None).then_inc(ids_scattered, 16)
            pool.wait_ge(ids_scattered, 2 * NT * 16)
            for h in range(2):
                pool.dma_start(yids_sb[h * SLOTS:(h + 1) * SLOTS, :].rearrange("r (b e) -> r b e", b=NBLK),
                               ids_dram.rearrange("(b r e) o -> r b (e o)", b=NBLK, e=NE)).then_inc(ids_loaded, 16)
            pool.wait_ge(ids_ready, 2)
            pool.wait_ge(h2_stored[0], 3 * 16)
            pool.wait_ge(h2_stored[1], 3 * 16)
            pool.wait_ge(oproj, 2 * NT)
            pool.wait_ge(counts_ready, 1)

            def await_count(what, count):
                pool.wait_ge(what, count)
                pool.sem_inc(pool_waited, 1)

            def gather(i, column, ready, count):
                pool.tensor_copy(id_cur[0:SLOTS, i:i + 1], ids_sb[0:SLOTS, bass.ds(column, 1)]).then_inc(ready, 1)
                await_count(ready, count)
                pool.indirect_dma_start(x_rows[i][0:SLOTS, :], None, h2_dram,
                                        bass.IndirectOffsetOnAxis(ap=id_cur[0:SLOTS, i:i + 1], axis=0)
                                        ).then_inc(rows_in[i], 16)

            def scatter(i, column, ready, count):
                pool.tensor_copy(yid_cur[:, i:i + 1], yids_sb[:, bass.ds(column, 1)]).then_inc(ready, 1)
                await_count(ready, count)
                pool.indirect_dma_start(y_dram, bass.IndirectOffsetOnAxis(ap=yid_cur[:, i:i + 1], axis=0), y_sb[i],
                                        None, bounds_check=4 * T - 1, oob_is_err=False).then_inc(y_stored[i], 16)

            def gather_main(g, s):
                e = g * RING + s
                if not isinstance(g, int) or e >= RING:
                    await_count(xeT_psum, e - RING + 1)
                gather(s % RING, e, id_ready, e + 1)

            def store_main(g, s):
                e = g * RING + s
                await_count(y_out, e + 1)
                scatter(s % 2, e, yid_ready, e + 1)

            EX = RING

            def rows_group(g):
                v = pool.value_load(packed_i[0:1, bass.ds(g, 1)], min_val=0, max_val=1 << 21)
                last_group = isinstance(g, int) and g == NE // RING - 1
                for s in range(RING):
                    e = g * RING + s
                    n, before = extras(v, s)
                    with pool.If(n > 0):
                        await_count(e_xeT_psum, before + 1)
                        gather(EX, NE + e, e_id, before + 1)
                    if not last_group or s == 0:
                        gather_main(g, s + RING - 1)
                    if not isinstance(g, int) or e >= 2:
                        store_main(g, s - 2)
                    with pool.If(n > 0):
                        with pool.Fori(0, n) as j:
                            c = before + j + 1
                            await_count(e_xeT_psum, c + 1)
                            with pool.If(j + 1 < n):
                                more = nc.s_assert_within(j, 0, NBLK - 3, skip_runtime_bounds_check_because="j + 1 < n < NBLK")
                                gather(EX, (more + 2) * NE + e, e_id, c + 1)
                            await_count(e_y, c + 1)
                            scatter(2, (j + 1) * NE + e, e_yid, c)

            for s in range(RING - 1):
                gather_main(0, s)
            rows_group(0)
            with pool.Fori(1, NE // RING - 1) as g:
                rows_group(g)
            rows_group(NE // RING - 1)
            for s in range(2):
                store_main(NE // RING - 1, RING - 2 + s)
            pool.wait_ge(y_stored[0], NE // 2 * 16)
            pool.wait_ge(y_stored[1], NE // 2 * 16)
            pool.sem_inc(all_stored, 1)

        @block.scalar
        def _(act):
            chain = [0]

            def link(ins):
                chain[0] += 1
                ins.then_inc(act_chain, 1)
                act.wait_ge(act_chain, chain[0])

            def square(t):
                act.wait_ge(x_in[t], 16)
                if t:
                    act.wait_ge(ss_ready, t)
                act.activation(junk, x_tok[:, t, :], ACT.Square, accum_out=ss[:, t:t + 1]).then_inc(ss_ready, 1)

            def proj_evac(mm):
                g, t = divmod(mm, 6)
                act.wait_ge(proj_done, mm + 1)
                act.wait_ge(rs_ready, t + 1)
                src = bank(mm % 2)[:, 0:GROUP_COLS[g]]
                if g == 0:
                    if t >= 3:
                        act.wait_ge(k_roped, t - 2)
                    dst = c_tok[t % 3]
                elif g < 3:
                    if mm >= 8:
                        act.wait_ge(dT_psum, mm - 7)
                    dst = qk_tok[mm % 2]
                else:
                    if t == 0:
                        act.wait_ge(up_done, 6)
                    dst = vd_tok[:, t, :]
                act.activation(dst, src, ACT.Copy, scale=rs[:, t:t + 1]).then_inc(proj_out, 1)

            def latent_square(t):
                act.wait_ge(proj_out, t + 1)
                if t:
                    act.wait_ge(ssc_ready, 2 * t)
                act.activation(junk_l[:, 0:Q_RANK], c_tok[t % 3][:, 0:Q_RANK], ACT.Square,
                               accum_out=ss_c[:, 2 * t:2 * t + 1]).then_inc(ssc_ready, 1)
                act.activation(junk_l[:, Q_RANK:Q_RANK + KV_RANK], c_tok[t % 3][:, Q_RANK:Q_RANK + KV_RANK],
                               ACT.Square, accum_out=ss_c[:, 2 * t + 1:2 * t + 2]).then_inc(ssc_ready, 1)

            def cT_evac(t):
                act.wait_ge(cT_psum, t + 1)
                if t >= 2:
                    act.wait_ge(up_done, t - 1)
                for j in range(3):
                    gain = gain_q[:, j:j + 1] if j < 2 else gain_kv
                    last = act.activation(cT[t % 2][:, j * P:(j + 1) * P], bank(2)[:, j * P:(j + 1) * P],
                                          ACT.Copy, scale=gain)
                last.then_inc(cT_ready, 1)

            def q_evac(t):
                act.wait_ge(up_done, t + 1)
                act.wait_ge(rsc_ready, t + 1)
                if t:
                    act.wait_ge(qkT_psum, t)
                both = psum[:, 3:5, :].rearrange("p b n -> p (b n)")[:, 0:HEADS * QK]
                act.activation(q_tok, both, ACT.Copy, scale=rs_c[:, 2 * t:2 * t + 1]).then_inc(q_out, 1)

            def kT_evac(t):
                act.wait_ge(qkT_psum, t + 1)
                act.activation(kT[0:QK, :, t * P:(t + 1) * P],
                               psum[0:QK, 5:7, :].rearrange("p b (h n) -> p (b h) n", n=P),
                               ACT.Copy).then_inc(kT_ready, 1)

            act.wait_ge(const_in, 3 * 16)
            square(0)
            square(1)
            act.wait_ge(lam_ready, 1)
            act.activation(lam_s[:, 2:4], lam_s[:, 0:2], ACT.Exp).then_inc(lam_e, 1)
            for i in range(25):
                if i + 1 < NT and i >= 1:
                    square(i + 1)
                if 3 <= i < 9:
                    kT_evac(i - 3)
                if i < 24:
                    proj_evac(i)
                if i < 6:
                    latent_square(i)
                if 2 <= i < 8:
                    q_evac(i - 2)
                if 1 <= i < 7:
                    cT_evac(i - 1)

            t_at = 0
            act.wait_ge(d_roped, 12)
            act.wait_ge(k_roped, 6)
            for i in range(N_UNITS + 4):
                if i < N_UNITS:
                    u = i
                    seq0, nt, kind, j, qt = UNITS[u]
                    act.wait_ge(nbias_ready, u + 1)
                    if u >= 3:
                        act.wait_ge(pT_psum, p_transposed(u - 3))
                    for a in range(2):
                        act.activation(p_tok[u % 3][:, a, 0:nt * P], bank(2 * (u % 2) + a)[:, 0:nt * P], ACT.Exp,
                                       bias=nbias[:, u % 4, a:a + 1], scale=MLA_SCALE if is_mla(u) else DIFF_SCALE,
                                       accum_out=l_sum[:, u % 6, a:a + 1]).then_inc(exps, 1)
                u = i - 2
                if 0 <= u < N_UNITS and is_mla(u):
                    nt = UNITS[u][1]
                    tau = TURN[("p", u, 1)]
                    act.wait_ge(pT_psum, tau + 1)
                    act.activation(pT[u % 2][:, 1, 0:nt, :],
                                   bank(4 + tau % 2)[:, 0:nt * P].rearrange("p (k n) -> p k n", n=P),
                                   ACT.Copy).then_inc(pT_act, 1)
                u = i - 3
                if 0 <= u < N_UNITS:
                    seq0, nt, kind, j, qt = UNITS[u]
                    act.wait_ge(pv_done, u + 1)
                    o = bank(6 + u % 2)[:, 0:P]
                    if is_mla(u):
                        act.activation(aT[:, j, (seq0 + qt) * P:(seq0 + qt + 1) * P], o, ACT.Copy).then_inc(o_mla, 1)
                    else:
                        b = batch(u)
                        if qt == 0 and b >= 2:
                            act.wait_ge(odT_ready, b - 1)
                        act.activation(od[b % 2][:, qt, :], o, ACT.Copy, scale=rl[:, u % 6, 0:1]).then_inc(o_diff, 1)
                        act.activation(junk_o, o, ACT.Square, scale=rl[:, u % 6, 0:1],
                                       accum_out=so[:, 4 * (b % 2) + qt:4 * (b % 2) + qt + 1]).then_inc(o_diff, 1)
                        act.wait_ge(o_diff, 2 * BEFORE[u] + 2)

            def ffn_square(t):
                act.wait_ge(x2_ready, 2 * t + 2)
                if t:
                    act.wait_ge(ss2_ready, t)
                act.activation(junk_c, x_tok[:, t, :], ACT.Square, accum_out=ss[:, t:t + 1]).then_inc(ss2_ready, 1)

            act.wait_ge(odT_ready, 8)
            for t in range(NT):
                ffn_square(t)
                act.wait_ge(h2T_psum, t + 1)
                if t:
                    act.wait_ge(logits, t)
                act.activation(h2T, psum[:, 4:6, :].rearrange("p b (c n) -> p (b c) n", n=P), ACT.Copy).then_inc(h2T_ready, 1)
                act.wait_ge(route_neg, t + 1)
                act.activation(r_g[:, 0:NG], logit[:, 0:NG], ACT.Exp, bias=r_small[:, 0:1],
                               accum_out=r_small[:, 1:2]).then_inc(act_chain, 1)
                chain[0] += 1
                act.activation(r_small[:, 3:4], r_small[:, 2:3], ACT.Exp).then_inc(route_exp, 1)

            act.wait_ge(counts_ready, 1)

            def further(g, s, v):
                e = g * RING + s
                n, before = extras(v, s)
                with act.If(n > 0):
                    with act.Fori(0, n) as j:
                        c = before + j + 1
                        act.wait_ge(e_gu, c)
                        act.activation(silu_t[2], bank(7)[:, 0:P], ACT.Silu).then_inc(e_silu, 1)
                        act.wait_ge(e_down, c)
                        act.activation(y_sb[2], bank(7), ACT.Copy).then_inc(e_y, 1)
                        act.wait_ge(y_stored[2], 16 * c)

            def y_evac(g, s):
                e = g * RING + s
                act.wait_ge(down_done, e + 1)
                if not isinstance(g, int) or e >= 2:
                    act.wait_ge(y_stored[s % 2], (g * 2 + s // 2) * 16)
                act.activation(y_sb[s % 2], bank(4 + s % 2), ACT.Copy).then_inc(y_out, 1)

            def act_group(g):
                v = act.value_load(packed_i[0:1, bass.ds(g, 1)], min_val=0, max_val=1 << 21)
                for s in range(RING):
                    e = g * RING + s
                    act.wait_ge(gu_done, e + 1)
                    if not isinstance(g, int) or e >= 2:
                        act.wait_ge(h_ready, e - 1)
                    act.activation(silu_t[s % 2], bank(1 + s % 2)[:, 0:P], ACT.Silu).then_inc(silu_done, 1)
                    if not isinstance(g, int) or e >= 1:
                        y_evac(g, s - 1)
                    further(g, s, v)

            act.sem_inc(e_y, 1)
            act_group(0)
            with act.Fori(1, NE // RING) as g:
                act_group(g)
            y_evac(NE // RING - 1, RING - 1)

            for t in range(NT):
                act.wait_ge(y_added, t + 1)
                if t:
                    act.wait_ge(ss3_ready, t)
                act.activation(junk_e, x_tok[:, t, :], ACT.Square, accum_out=ss[:, t:t + 1]).then_inc(ss3_ready, 1)

        @block.vector
        def _(dve):
            chain = [0]

            def link(ins):
                chain[0] += 1
                ins.then_inc(dve_chain, 1)
                dve.wait_ge(dve_chain, chain[0])

            def rsqrt(dst, src, n, scale):
                x, hx, t = (nw[:, i * 8:i * 8 + n] for i in range(3))
                link(dve.tensor_scalar(x, src, scale, EPS, ALU.mult, ALU.add))
                link(dve.tensor_scalar(t.bitcast(u32), x.bitcast(u32), 1, None, ALU.logical_shift_right))
                link(dve.tensor_scalar(dst.bitcast(i32), t.bitcast(i32), -1.0, float(MAGIC), ALU.mult, ALU.add))
                link(dve.tensor_scalar(hx, x, -0.5, None, ALU.mult))
                for step in range(3):
                    link(dve.tensor_tensor(t, dst, dst, ALU.mult))
                    link(dve.tensor_tensor(t, t, hx, ALU.mult))
                    last = dve.scalar_tensor_tensor(dst, t, 1.5, dst, ALU.add, ALU.mult)
                    if step < 2:
                        link(last)
                return last

            def gain(t):
                dve.wait_ge(xT_in[t], 16)
                dve.tensor_tensor(xgT[:, t, :, :], xgT[:, t, :, :],
                                  gain_in.unsqueeze(2).to_broadcast([P, DC, P]), ALU.mult).then_inc(xg_ready, 1)

            def kv_evac(t):
                dve.wait_ge(up_done, t + 1)
                dve.wait_ge(rsc_ready, t + 1)
                if t:
                    dve.wait_ge(qkT_psum, t)
                kv = psum[:, 5:7, :].rearrange("p b (h n) -> p (b h) n", n=P)
                dve.tensor_scalar(k_tok.rearrange("p (h n) -> p h n", h=HEADS)[:, :, 0:NOPE], kv[:, :, 0:NOPE],
                                  rs_c[:, 2 * t + 1:2 * t + 2], None, ALU.mult)
                dve.tensor_scalar(v_tok[:, t, :].rearrange("p (h n) -> p h n", h=HEADS), kv[:, :, NOPE:P],
                                  rs_c[:, 2 * t + 1:2 * t + 2], None, ALU.mult).then_inc(kv_out, 1)

            def latent_norm(t):
                dve.wait_ge(ssc_ready, 2 * t + 2)
                link(dve.tensor_scalar(ss_c[:, 2 * t:2 * t + 1], ss_c[:, 2 * t:2 * t + 1], KV_RANK / Q_RANK, None, ALU.mult))
                rsqrt(rs_c[:, 2 * t:2 * t + 2], ss_c[:, 2 * t:2 * t + 2], 2, 1.0 / KV_RANK).then_inc(rsc_ready, 1)

            def norm_x(t):
                dve.wait_ge(ss_ready, t + 1)
                rsqrt(rs[:, t:t + 1], ss[:, t:t + 1], 1, 1.0 / D).then_inc(rs_ready, 1)
                dve.wait_ge(rs_ready, t + 1)

            dve.wait_ge(gain_loaded, 16)
            gain(0)
            gain(1)
            norm_x(0)
            norm_x(1)
            dve.wait_ge(lam_loaded, 4 * 16)
            for i in range(2):
                link(dve.tensor_tensor(lam_t, lam_in[:, 2 * i * DD:(2 * i + 1) * DD],
                                       lam_in[:, (2 * i + 1) * DD:(2 * i + 2) * DD], ALU.mult))
                link(dve.reduce_sum(lam_s[:, i:i + 1], lam_t, X_))
            dve.sem_inc(lam_ready, 1)
            for i in range(25):
                if 1 <= i < NT - 1:
                    gain(i + 1)
                    norm_x(i + 1)
                if 3 <= i < 9:
                    t = i - 3
                    dve.wait_ge(qkT_psum, t + 1)
                    dve.tensor_copy(qT[0:QK, :, t * P:(t + 1) * P],
                                    psum[0:QK, 3:5, :].rearrange("p b (h n) -> p (b h) n", n=P)).then_inc(qT_ready, 1)
                if i < 6:
                    latent_norm(i)
                    dve.wait_ge(rsc_ready, i + 1)
                if i == 1:
                    dve.wait_ge(lam_e, 1)
                    link(dve.tensor_tensor(neglam, lam_s[:, 3:4], lam_s[:, 2:3], ALU.subtract))
                    link(dve.tensor_scalar(neglam, neglam, LAMBDA_INIT, None, ALU.subtract))
                    link(dve.tensor_scalar(gain_sub, gain_sub, 1.0 - LAMBDA_INIT, None, ALU.mult))
                mm = i - 1
                if 6 <= mm < 18:
                    d, t = mm - 6, mm % 6
                    dve.wait_ge(dT_psum, d + 1)
                    dst = qdT if d < 6 else kdT
                    dve.tensor_copy(dst[:, :, t * P:(t + 1) * P],
                                    bank(7).rearrange("p (h n) -> p h n", n=P)).then_inc(dT_ready, 1)
                if 2 <= i < 8:
                    kv_evac(i - 2)

            dve.wait_ge(proj_out, 24)
            dve.wait_ge(q_roped, 6)
            dve.wait_ge(k_roped, 6)
            dve.wait_ge(d_roped, 12)
            dve.wait_ge(cT_ready, 6)
            dve.wait_ge(up_done, 6)
            for i in range(N_UNITS + 6):
                if i < N_UNITS:
                    u = i
                    nt = UNITS[u][1]
                    for a in range(2):
                        dve.wait_ge(scores, 2 * u + a + 1)
                        if a == 0 and u >= 4:
                            dve.wait_ge(exps, 2 * (u - 4) + 2)
                        dve.reduce_max(mx[:, u % 4, a:a + 1], bank(2 * (u % 2) + a)[:, 0:nt * P], X_).then_inc(dve_chain, 1)
                        chain[0] += 1
                    dve.wait_ge(dve_chain, chain[0])
                    dve.tensor_scalar(nbias[:, u % 4, :], mx[:, u % 4, :], -(MLA_SCALE if is_mla(u) else DIFF_SCALE),
                                      None, ALU.mult).then_inc(nbias_ready, 1)
                u = i - 2
                if 0 <= u < N_UNITS:
                    nt = UNITS[u][1]
                    tau = TURN[("p", u, 0)]
                    dve.wait_ge(pT_psum, tau + 1)
                    dve.tensor_copy(pT[u % 2][:, 0, 0:nt, :],
                                    bank(4 + tau % 2)[:, 0:nt * P].rearrange("p (k n) -> p k n", n=P)
                                    ).then_inc(pT_dve, 1)
                u = i
                if u < N_UNITS:
                    nt = UNITS[u][1]
                    dve.wait_ge(exps, 2 * u + 2)
                    if u >= 6 and is_mla(u - 6):
                        dve.wait_ge(p_normed, 2 * BEFORE[u - 6] + 2)
                    dve.reciprocal(rl[:, u % 6, :], l_sum[:, u % 6, :]).then_inc(rl_ready, 1)
                    dve.wait_ge(rl_ready, u + 1)
                    if not is_mla(u):
                        link(dve.scalar_tensor_tensor(cmix[:, 0:1], l_sum[:, u % 6, 0:1], neglam, rl[:, u % 6, 1:2], ALU.mult, ALU.mult))
                        p = p_tok[u % 3]
                        dve.scalar_tensor_tensor(p[:, 0, 0:nt * P], p[:, 1, 0:nt * P], cmix[:, 0:1], p[:, 0, 0:nt * P],
                                                 ALU.mult, ALU.add).then_inc(p_mixed, 1)
                        dve.wait_ge(p_mixed, BEFORE[u] + 1)
                u = i - 4
                if 0 <= u < N_UNITS and ends_batch(u):
                    b, nt = batch(u), UNITS[u][1]
                    dve.wait_ge(o_diff, 2 * BEFORE[u] + 2)
                    rsqrt(ro[:, 4 * (b % 2):4 * (b % 2) + nt], so[:, 4 * (b % 2):4 * (b % 2) + nt], nt,
                          1.0 / (2 * DD)).then_inc(ro_ready, 1)
                    dve.wait_ge(ro_ready, b + 1)
                    for qt in range(nt):
                        o = od[b % 2][:, qt, :]
                        last = dve.tensor_scalar(o, o, ro[:, 4 * (b % 2) + qt:4 * (b % 2) + qt + 1], None, ALU.mult)
                    last.then_inc(od_scaled, 1)
                u = i - 5
                if 0 <= u < N_UNITS and ends_batch(u):
                    seq0, nt, kind, j, qt = UNITS[u]
                    tau = TURN[("o", u, 0)]
                    dve.wait_ge(pT_psum, tau + 1)
                    dve.tensor_scalar(aT[:, 4 + j, seq0 * P:(seq0 + nt) * P], bank(4 + tau % 2)[:, 0:nt * P], gain_sub, None,
                                      ALU.mult).then_inc(odT_ready, 1)

            dve.wait_ge(odT_ready, 8)
            dve.wait_ge(o_mla, N_UNITS // 2)
            dve.wait_ge(pv_done, N_UNITS)
            dve.wait_ge(p_normed, N_UNITS)
            dve.memset(ones, 1.0).then_inc(ones_ready, 1)

            def residual(t):
                for h in range(2):
                    dve.wait_ge(oproj, 2 * t + h + 1)
                    x = x_tok[:, t, h * 512:(h + 1) * 512]
                    dve.tensor_tensor(x, x, bank(2 * (t % 2) + h), ALU.add).then_inc(x2_ready, 1)

            def ffn_norm(t):
                dve.wait_ge(ss2_ready, t + 1)
                link(rsqrt(rs[:, t:t + 1], ss[:, t:t + 1], 1, 1.0 / D))
                if t == 0:
                    dve.wait_ge(gffn_in, 16)
                if t >= 2:
                    dve.wait_ge(h2_stored[t % 2], 16 * (t // 2))
                    dve.wait_ge(h2T_psum, t - 1)
                dve.scalar_tensor_tensor(h2[t % 2].rearrange("n (c p) -> n c p", c=DC),
                                         x_tok[:, t, :].rearrange("n (p c) -> n c p", c=DC), rs[:, t:t + 1],
                                         gain_ffn.rearrange("n (p c) -> n c p", c=DC), ALU.mult, ALU.mult).then_inc(h2_ready, 1)

            def first_max(mask, key, values, rev, width, m):
                link(dve.tensor_scalar(key, values, m, None, ALU.is_equal))
                link(dve.tensor_tensor(key, key, rev, ALU.mult))
                link(dve.reduce_max(r_small[:, 8:9], key, X_))
                return dve.tensor_scalar(mask, key, r_small[:, 8:9], None, ALU.is_equal)

            def route(t):
                dve.wait_ge(logits, t + 1)
                if t == 0:
                    dve.wait_ge(router_in, 4 * 16)
                link(dve.tensor_tensor(logit, bank(6)[:, 0:NG + NE], bias_r, ALU.add))
                gl, el = logit[:, 0:NG], logit[:, NG:NG + NE]
                key_g, mask_g = r_g[:, NG:2 * NG], r_g[:, 2 * NG:3 * NG]
                gmax, ngmax, diff = r_small[:, 4:5], r_small[:, 0:1], r_small[:, 2:3]
                link(dve.reduce_max(gmax, gl, X_))
                link(dve.tensor_scalar(ngmax, gmax, -1.0, None, ALU.mult))
                link(first_max(mask_g, key_g, gl, const("rev_g"), NG, gmax))
                link(dve.tensor_scalar(key_g, mask_g, 1e30, -1e30, ALU.mult, ALU.add))
                masked, key, second = r_e[:, 0:NE], r_e[:, NE:2 * NE], r_e[:, 2 * NE:3 * NE]
                link(dve.tensor_tensor(masked.rearrange("p (g e) -> p g e", g=NG), el.rearrange("p (g e) -> p g e", g=NG),
                                       key_g.unsqueeze(2).to_broadcast([P, NG, EPG]), ALU.add))
                link(dve.reduce_max(r_small[:, 5:6], masked, X_))
                link(first_max(m1_all[:, t, :], key, masked, const("rev_e"), NE, r_small[:, 5:6]))
                link(dve.scalar_tensor_tensor(second, m1_all[:, t, :], -3e38, masked, ALU.mult, ALU.add))
                link(dve.reduce_max(r_small[:, 6:7], second, X_))
                link(first_max(m2_all[:, t, :], key, second, const("rev_e"), NE, r_small[:, 6:7]))
                link(dve.tensor_tensor(diff, r_small[:, 6:7], r_small[:, 5:6], ALU.subtract))
                dve.sem_inc(route_neg, 1)
                if t == 0:
                    link(dve.tensor_copy(macc[:, 0, :], m1_all[:, 0, :]))
                else:
                    link(dve.tensor_tensor(macc[:, t, :], macc[:, t - 1, :], m1_all[:, t, :], ALU.add))
                link(dve.tensor_tensor(m12[:, t, :], m1_all[:, t, :], m2_all[:, t, :], ALU.add))
                dve.tensor_tensor(macc[:, t, :], macc[:, t, :], m2_all[:, t, :], ALU.add).then_inc(masks, 1)
                dve.wait_ge(route_exp, t + 1)
                link(dve.tensor_scalar(r_small[:, 7:8], r_small[:, 3:4], 1.0, None, ALU.add))
                link(dve.tensor_tensor(r_small[:, 7:8], r_small[:, 7:8], r_small[:, 1:2], ALU.mult))
                link(dve.reciprocal(gates[:, 2 * t:2 * t + 1], r_small[:, 7:8]))
                link(dve.tensor_tensor(gates[:, 2 * t + 1:2 * t + 2], gates[:, 2 * t:2 * t + 1], r_small[:, 3:4], ALU.mult))

            def slots(t):
                dve.wait_ge(ranks, t + 1)
                rank = bank(7)[:, 0:NE]
                key, prod = r_e[:, NE:2 * NE], r_e[:, 3 * NE:4 * NE]
                link(dve.scalar_tensor_tensor(key, rank, float(NE), const("iota_e"), ALU.mult, ALU.add))
                for i, mask in enumerate((m1_all, m2_all)):
                    link(dve.tensor_tensor(prod, key, mask[:, t, :], ALU.mult))
                    link(dve.reduce_sum(slot_f[:, i:i + 1], prod, X_))
                dve.tensor_copy(slot_u[:, 2 * t:2 * t + 2], slot_f).then_inc(slots_ready, 1)
                dve.wait_ge(slots_ready, t + 1)

            residual(0)
            for t in range(NT):
                ffn_norm(t)
                if t + 1 < NT:
                    residual(t + 1)
                route(t)
                if t:
                    slots(t - 1)
            slots(NT - 1)
            dve.wait_ge(counts_psum, 1)
            link(dve.tensor_copy(cnt[0:1, :], bank(6)[0:1, 64:64 + NE]))
            ov = over[0:1, :].rearrange("o (e k) -> o e k", e=NE)
            link(dve.tensor_tensor(ov, cnt[0:1, :].unsqueeze(2).to_broadcast([1, NE, NBLK - 1]),
                                   const("steps")[0:1, :].unsqueeze(1).to_broadcast([1, NE, NBLK - 1]), ALU.is_gt))
            link(dve.reduce_sum(extra[0:1, :], ov, X_))
            link(dve.tensor_tensor(cnt[0:1, :].rearrange("o (g s) -> o g s", s=RING),
                                   extra[0:1, :].rearrange("o (g s) -> o g s", s=RING),
                                   const("pack4")[0:1, :].unsqueeze(1).to_broadcast([1, NE // RING, RING]), ALU.mult))
            link(dve.reduce_sum(r_e[0:1, 0:8], cnt[0:1, :].rearrange("o (g s) -> o g s", s=RING), X_))
            link(dve.reduce_sum(r_e[0:1, 8:16], extra[0:1, :].rearrange("o (g s) -> o g s", s=RING), X_))
            link(dve.tensor_tensor(pk[0:1, :].rearrange("o (g h) -> o g h", g=8),
                                   const("before_g")[0:1, :].rearrange("o (g h) -> o g h", g=8),
                                   r_e[0:1, 8:16].unsqueeze(1).to_broadcast([1, 8, 8]), ALU.mult))
            link(dve.reduce_sum(r_e[0:1, 16:24], pk[0:1, :].rearrange("o (g h) -> o g h", g=8), X_))
            link(dve.tensor_tensor(packed_i[0:1, :], r_e[0:1, 0:8], r_e[0:1, 16:24], ALU.add))
            dve.sem_inc(counts_ready, 1)
            dve.wait_ge(ids_loaded, 32)
            link(dve.tensor_scalar(ids_sb, yids_sb, 1, None, ALU.logical_shift_right))
            dve.tensor_scalar(ids_sb, ids_sb, float(T - 1), None, ALU.min).then_inc(ids_ready, 1)
            dve.tensor_scalar(yids_sb, yids_sb, 2.0, const("map_rows")[:, 1:2], ALU.mult, ALU.add).then_inc(ids_ready, 1)

            def dve_group(g):
                v = dve.value_load(packed_i[0:1, bass.ds(g, 1)], min_val=0, max_val=1 << 21)
                last_group = isinstance(g, int) and g == NE // RING - 1
                for s in range(RING):
                    e = g * RING + s
                    n, before = extras(v, s)
                    dve.wait_ge(silu_done, e + 1)
                    dve.tensor_tensor(h_tok[s % 2], silu_t[s % 2], bank(1 + s % 2)[:, P:2 * P], ALU.mult).then_inc(h_ready, 1)
                    if not (last_group and s == RING - 1):
                        dve.wait_ge(xeT_psum, e + 2)
                        dve.tensor_copy(x_eT[(s + 1) % 2], bank(0).rearrange("p (c n) -> p c n", c=DC)).then_inc(xeT_ready, 1)
                    dve.wait_ge(hT_psum, e + 1)
                    if not isinstance(g, int) or e >= 1:
                        dve.wait_ge(down_done, e)
                    dve.tensor_copy(h_T[0], bank(3)[:, 0:P]).then_inc(hT_ready, 1)
                    with dve.If(n > 0):
                        with dve.Fori(0, n) as j:
                            c = before + j + 1
                            dve.wait_ge(e_xeT_psum, c + 1)
                            dve.tensor_copy(x_eT[2], bank(6).rearrange("p (c n) -> p c n", c=DC)).then_inc(e_xeT, 1)
                            dve.wait_ge(e_silu, c)
                            dve.tensor_tensor(h_tok[2], silu_t[2], bank(7)[:, P:2 * P], ALU.mult).then_inc(e_h, 1)
                            dve.wait_ge(e_hT_psum, c)
                            dve.tensor_copy(h_T[1], bank(6)[:, 0:P]).then_inc(e_hT, 1)

            dve.wait_ge(xeT_psum, 1)
            dve.tensor_copy(x_eT[0], bank(0).rearrange("p (c n) -> p c n", c=DC)).then_inc(xeT_ready, 1)
            dve_group(0)
            with dve.Fori(1, NE // RING - 1) as g:
                dve_group(g)
            dve_group(NE // RING - 1)

            def final(t):
                dve.wait_ge(ss3_ready, t + 1)
                link(rsqrt(rs[:, t:t + 1], ss[:, t:t + 1], 1, 1.0 / D))
                if t == 0:
                    dve.wait_ge(gfin_in, 16)
                dve.scalar_tensor_tensor(y_rows[:, 2 * t, :], x_tok[:, t, :], rs[:, t:t + 1], gain_fin, ALU.mult,
                                         ALU.mult).then_inc(final_ready, 1)

            for t in range(NT):
                dve.wait_ge(yrows_in[t], 16)
                x = x_tok[:, t, :]
                link(dve.scalar_tensor_tensor(x, y_rows[:, 2 * t, :], gates[:, 2 * t:2 * t + 1], x, ALU.mult, ALU.add))
                dve.scalar_tensor_tensor(x, y_rows[:, 2 * t + 1, :], gates[:, 2 * t + 1:2 * t + 2], x, ALU.mult,
                                         ALU.add).then_inc(y_added, 1)
                if t:
                    final(t - 1)
            final(NT - 1)

        @block.tensor
        def _(pe):
            def proj(mm, half):
                g, t = divmod(mm, 6)
                if half == 0:
                    pe.wait_ge(win_in[g], 16)
                    pe.wait_ge(xg_ready, t + 1)
                    if mm >= 2:
                        pe.wait_ge(proj_out, mm - 1)
                w = group_w(g)
                for c in range(4 * half, 4 * half + 4):
                    last = nc.tensor.matmul(bank(mm % 2)[:, 0:GROUP_COLS[g]], xgT[:, t, c, :], w[:, c, :],
                                            start=(c == 0), stop=(c == DC - 1))
                if half == 1:
                    last.then_inc(proj_done, 1)

            def latent_transpose(t):
                pe.wait_ge(proj_out, t + 1)
                if t:
                    pe.wait_ge(cT_ready, t)
                else:
                    pe.wait_ge(const_in, 3 * 16)
                for j in range(3):
                    last = nc.tensor.transpose(bank(2)[:, j * P:(j + 1) * P], c_tok[t % 3][:, j * P:(j + 1) * P], ident)
                last.then_inc(cT_psum, 1)

            def up(t):
                pe.wait_ge(cT_ready, t + 1)
                pe.wait_ge(wup_in, 32)
                if t:
                    pe.wait_ge(qT_ready, t)
                    pe.wait_ge(kT_ready, t)
                for b, a, n in ((3, 0, 512), (4, 512, 256)):
                    for c in range(2):
                        nc.tensor.matmul(bank(b)[:, 0:n], cT[t % 2][:, c * P:(c + 1) * P], w_uq_sb[:, c, a:a + n],
                                         start=(c == 0), stop=(c == 1))
                for h in range(2):
                    last = nc.tensor.matmul(bank(5 + h), cT[t % 2][:, 2 * P:3 * P], w_ukv_sb[:, h * 512:(h + 1) * 512],
                                            start=True, stop=True)
                last.then_inc(up_done, 1)

            def head_transpose(t):
                pe.wait_ge(q_roped, t + 1)
                pe.wait_ge(kv_out, t + 1)
                pe.wait_ge(k_roped, t + 1)
                for b, src in ((3, q_tok), (5, k_tok)):
                    for h in range(HEADS):
                        last = nc.tensor.transpose(bank(b + h // 4)[0:QK, (h % 4) * P:(h % 4 + 1) * P],
                                                   src[:, h * QK:(h + 1) * QK], ident)
                last.then_inc(qkT_psum, 1)

            def diff_transpose(mm):
                d = mm - 6
                pe.wait_ge(d_roped, d + 1)
                if d:
                    pe.wait_ge(dT_ready, d)
                for h in range(DH):
                    last = nc.tensor.transpose(bank(7)[:, h * P:(h + 1) * P], qk_tok[mm % 2][:, h * P:(h + 1) * P], ident)
                last.then_inc(dT_psum, 1)

            for i in range(25):
                if i < 24:
                    proj(i, 0)
                if 3 <= i < 9:
                    head_transpose(i - 3)
                if 6 <= i - 1 < 18:
                    diff_transpose(i - 1)
                if i < 24:
                    proj(i, 1)
                if 2 <= i < 8:
                    up(i - 2)
                if 1 <= i < 7:
                    latent_transpose(i - 1)

            def score(u):
                seq0, nt, kind, j, qt = UNITS[u]
                tok = slice((seq0 + qt) * P, (seq0 + qt + 1) * P)
                keys = slice(seq0 * P, (seq0 + nt) * P)
                if u >= 2:
                    pe.wait_ge(exps, 2 * (u - 2) + 2)
                if not is_mla(u):
                    pe.wait_ge(qpad_ready, 2 * BEFORE[u] + 2)
                for a in range(2):
                    if is_mla(u):
                        l, r = qT[0:QK, 2 * j + a, tok], kT[0:QK, 2 * j + a, keys]
                    else:
                        l, r = q_pad[BEFORE[u] % 2][:, a, :], kdT[:, j, keys]
                    nc.tensor.matmul(bank(2 * (u % 2) + a)[:, 0:nt * P], l, r, start=True, stop=True).then_inc(scores, 1)

            def wait_bank_read(tau):
                if tau >= 2:
                    kind, v, a = TRANSPOSES[tau - 2]
                    if kind == "o":
                        pe.wait_ge(odT_ready, batch(v) + 1)
                    elif a:
                        pe.wait_ge(pT_act, BEFORE[v] + 1)
                    else:
                        pe.wait_ge(pT_dve, v + 1)

            def transpose_p(u):
                nt = UNITS[u][1]
                if is_mla(u):
                    pe.wait_ge(p_normed, 2 * BEFORE[u] + 2)
                else:
                    pe.wait_ge(p_mixed, BEFORE[u] + 1)
                for a in range(2 if is_mla(u) else 1):
                    tau = TURN[("p", u, a)]
                    wait_bank_read(tau)
                    for kt in range(nt):
                        last = nc.tensor.transpose(bank(4 + tau % 2)[:, kt * P:(kt + 1) * P],
                                                   p_tok[u % 3][:, a, kt * P:(kt + 1) * P], ident)
                    last.then_inc(pT_psum, 1)

            def attend(u):
                seq0, nt, kind, j, qt = UNITS[u]
                pe.wait_ge(pT_dve, u + 1)
                if is_mla(u):
                    pe.wait_ge(pT_act, BEFORE[u] + 1)
                if u >= 2:
                    if is_mla(u):
                        pe.wait_ge(o_mla, BEFORE[u - 2] + 1)
                    else:
                        pe.wait_ge(o_diff, 2 * BEFORE[u - 2] + 2)
                o = bank(6 + u % 2)[:, 0:P]
                for kt in range(nt):
                    st = dict(start=(kt == 0), stop=(kt == nt - 1))
                    if is_mla(u):
                        for a in range(2):
                            last = nc.tensor.matmul(o[a * VD:(a + 1) * VD, :],
                                                    v_tok[:, seq0 + kt, (2 * j + a) * VD:(2 * j + a + 1) * VD],
                                                    pT[u % 2][:, a, kt, :], **st)
                    else:
                        last = nc.tensor.matmul(o, pT[u % 2][:, 0, kt, :], vd_tok[:, seq0 + kt, j * P:(j + 1) * P], **st)
                last.then_inc(pv_done, 1)

            def transpose_o(u):
                b, nt = batch(u), UNITS[u][1]
                pe.wait_ge(od_scaled, b + 1)
                tau = TURN[("o", u, 0)]
                wait_bank_read(tau)
                for qt in range(nt):
                    last = nc.tensor.transpose(bank(4 + tau % 2)[:, qt * P:(qt + 1) * P], od[b % 2][:, qt, :], ident)
                last.then_inc(pT_psum, 1)

            pe.wait_ge(qT_ready, 6)
            pe.wait_ge(kT_ready, 6)
            pe.wait_ge(dT_ready, 12)
            pe.wait_ge(proj_out, 24)
            for i in range(N_UNITS + 6):
                if i < N_UNITS:
                    score(i)
                if 0 <= i - 2 < N_UNITS:
                    transpose_p(i - 2)
                if 0 <= i - 3 < N_UNITS:
                    attend(i - 3)
                u = i - 5
                if 0 <= u < N_UNITS and ends_batch(u):
                    transpose_o(u)

            def out_half(t, h):
                if t >= 2:
                    pe.wait_ge(x2_ready, 2 * (t - 2) + h + 1)
                for c in range(DC):
                    last = nc.tensor.matmul(bank(2 * (t % 2) + h), aT[:, c, t * P:(t + 1) * P],
                                            w_out_sb[:, c, h * 512:(h + 1) * 512], start=(c == 0), stop=(c == DC - 1))
                last.then_inc(oproj, 1)

            def h2_transpose(t):
                pe.wait_ge(h2_ready, t + 1)
                if t:
                    pe.wait_ge(h2T_ready, t)
                for c in range(DC):
                    last = nc.tensor.transpose(bank(4 + c // 4)[:, (c % 4) * P:(c % 4 + 1) * P],
                                               h2[t % 2][:, c * P:(c + 1) * P], ident)
                last.then_inc(h2T_psum, 1)

            def router(t):
                pe.wait_ge(h2T_ready, t + 1)
                if t == 0:
                    pe.wait_ge(router_in, 4 * 16)
                else:
                    pe.wait_ge(masks, t)
                for c in range(DC):
                    last = nc.tensor.matmul(bank(6)[:, 0:NG + NE], h2T[:, c, :], w_r[:, c, :],
                                            start=(c == 0), stop=(c == DC - 1))
                last.then_inc(logits, 1)

            def rank(t):
                pe.wait_ge(masks, t + 1)
                if t:
                    pe.wait_ge(slots_ready, t)
                out = bank(7)[:, 0:NE]
                last = nc.tensor.matmul(out, const("upper"), m12[:, t, :], start=True, stop=(t == 0))
                if t:
                    last = nc.tensor.matmul(out, ones, macc[:, t - 1, :], start=False, stop=True)
                last.then_inc(ranks, 1)

            pe.wait_ge(wout_in, 16)
            pe.wait_ge(odT_ready, 8)
            pe.wait_ge(o_mla, N_UNITS // 2)
            pe.wait_ge(ones_ready, 1)
            for t in range(NT + 1):
                if t < NT:
                    out_half(t, 0)
                if t >= 1:
                    if t >= 2:
                        rank(t - 2)
                    h2_transpose(t - 1)
                if t < NT:
                    out_half(t, 1)
                if t >= 1:
                    router(t - 1)
            rank(NT - 1)
            nc.tensor.matmul(bank(6)[:, 64:64 + NE], ones, macc[:, NT - 1, :], start=True, stop=True).then_inc(counts_psum, 1)

            def rows_transpose(b, i, chunks):
                for c in chunks:
                    last = nc.tensor.transpose(bank(b)[:, c * SLOTS:(c + 1) * SLOTS],
                                               x_rows[i][0:SLOTS, c * P:(c + 1) * P], ident[0:SLOTS, 0:SLOTS])
                return last

            def gate_up(b, i, s):
                w = ring[s][:, 0:4096].rearrange("p (g c n) -> p g c n", g=2, c=DC)
                for c in range(DC):
                    for h in range(2):
                        last = nc.tensor.matmul(bank(b)[h * SLOTS:(h + 1) * SLOTS, 0:2 * P].rearrange("p (g n) -> p g n", g=2),
                                                x_eT[i][:, c, :], w[:, :, c, h * P:(h + 1) * P],
                                                start=(c == 0), stop=(c == DC - 1))
                return last

            def down(b, hT, s):
                w = ring[s][:, 4096:6144].rearrange("p (j n) -> p j n", j=2)
                for j in range(2):
                    for h in range(2):
                        last = nc.tensor.matmul(bank(b)[h * SLOTS:(h + 1) * SLOTS, :], hT[:, j * SLOTS:(j + 1) * SLOTS],
                                                w[:, j, h * 512:(h + 1) * 512], start=(j == 0), stop=(j == 1))
                return last

            def await_rows(what, count):
                pe.wait_ge(what, count)
                pe.sem_inc(pe_waited, 1)

            def pe_group(g):
                v = pe.value_load(packed_i[0:1, bass.ds(g, 1)], min_val=0, max_val=1 << 21)
                last_group = isinstance(g, int) and g == NE // RING - 1
                for s in range(RING):
                    e = g * RING + s
                    pe.wait_ge(w_loaded[s], 48 * (g + 1))
                    first = isinstance(g, int) and e == 0
                    pe.wait_ge(xeT_ready, e + 1)
                    gate_up(1 + s % 2, s % 2, s).then_inc(gu_done, 1)
                    if not (last_group and s == RING - 1):
                        await_rows(rows_in[(s + 1) % RING], 16 * (g + (s + 1) // RING + 1))
                        rows_transpose(0, (s + 1) % RING, range(DC)).then_inc(xeT_psum, 1)
                    if not first:
                        down_main(g, s - 1)
                    pe.wait_ge(h_ready, e + 1)
                    nc.tensor.transpose(bank(3)[:, 0:P], h_tok[s % 2], ident).then_inc(hT_psum, 1)
                    n, before = extras(v, s)
                    with pe.If(n > 0):
                        with pe.Fori(0, n) as j:
                            c = before + j + 1
                            await_rows(rows_in[RING], 16 * c)
                            rows_transpose(6, RING, range(DC)).then_inc(e_xeT_psum, 1)
                            pe.wait_ge(e_xeT, c)
                            pe.wait_ge(e_y, c)
                            gate_up(7, 2, s).then_inc(e_gu, 1)
                            pe.wait_ge(e_h, c)
                            nc.tensor.transpose(bank(6)[:, 0:P], h_tok[2], ident).then_inc(e_hT_psum, 1)
                            pe.wait_ge(e_hT, c)
                            down(7, h_T[1], s).then_inc(e_down, 1)

            def down_main(g, s):
                e = g * RING + s
                pe.wait_ge(hT_ready, e + 1)
                if not isinstance(g, int) or e >= 2:
                    pe.wait_ge(y_out, e - 1)
                down(4 + s % 2, h_T[0], s % RING).then_inc(down_done, 1)

            pe.sem_inc(e_xeT_psum, 1)
            pe.wait_ge(rows_in[0], 16)
            pe.wait_ge(counts_ready, 1)
            rows_transpose(0, 0, range(DC)).then_inc(xeT_psum, 1)
            pe_group(0)
            with pe.Fori(1, NE // RING - 1) as g:
                pe_group(g)
            pe_group(NE // RING - 1)
            down_main(NE // RING - 1, RING - 1)


WEIGHTS = ["attn_norm", "w_in", "w_uq", "w_ukv", "diff_lq1", "diff_lk1", "diff_lq2",
           "diff_lk2", "w_out", "ffn_norm", "router_group", "router_group_bias", "router_expert",
           "router_expert_bias", "w_gate", "w_up", "w_down", "final_norm"]


def kernel(**inputs):
    import concourse.bacc as _bacc
    from concourse.bass_utils import run_bass_kernel_spmd as _run

    nc = _bacc.Bacc("TRN2", target_bir_lowering=False, num_devices=1)
    x = np.concatenate([np.asarray(inputs["x_prompt"])[0], np.asarray(inputs["x_sample"])[0]], axis=0)
    arrays = {
        "x": np.ascontiguousarray(x),
        "xT": np.ascontiguousarray(x.reshape(NT, P, P, DC).transpose(2, 0, 3, 1)),
        "consts": constants(),
        "pairid": np.ascontiguousarray(np.arange(2 * T, dtype=np.uint32).reshape(NT, P, 2).transpose(1, 0, 2).reshape(P, 2 * NT)),
    }
    arrays["gains"] = np.ascontiguousarray(np.concatenate(
        [np.asarray(inputs[n]).reshape(-1, P) for n in ("q_norm", "kv_norm", "diff_subln")], axis=0).T)
    for n in WEIGHTS:
        arrays[n] = np.ascontiguousarray(np.asarray(inputs[n]))
    arrays["w_in"] = arrays["w_in"].reshape(D, -1)
    A = {n: nc.dram_tensor(n, a.shape, mybir.dt.from_np(a.dtype), kind="ExternalInput").ap() for n, a in arrays.items()}
    for n, s in (("y_prompt", S_PROMPT), ("y_sample", S_SAMPLE)):
        A[n] = nc.dram_tensor(n, (1, s, D), mybir.dt.float32, kind="ExternalOutput").ap()
    build(nc, A)
    r = _run(nc, [arrays], core_ids=[0])
    return r.results[0]["y_prompt"], r.results[0]["y_sample"]
```

```python
import math
from contextlib import ExitStack

import numpy as np
import concourse.bass as bass
from concourse import mybir

P = 128
D = 1024
S_PROMPT, S_SAMPLE = 256, 512
T = S_PROMPT + S_SAMPLE
NT = T // P
DC = D // P
Q_RANK, KV_RANK, ROPE = 256, 128, 32
HEADS, NOPE, VD = 8, 64, 64
QK = NOPE + ROPE
DH, DD = 4, 64
ROT = DD // 4
LATENT = Q_RANK + KV_RANK + ROPE
GROUP_COLS = [LATENT, DH * 2 * DD, DH * 2 * DD, DH * 2 * DD]
GROUP_AT = [0, LATENT, LATENT + 512, LATENT + 1024]
NG, EPG = 4, 8
NE = NG * EPG
FF = 256
EPS = 1e-6
THETA = 500000.0
LAMBDA_INIT = 0.8 - 0.6 * math.exp(-0.3 * 0)
MLA_SCALE = QK ** -0.5
DIFF_SCALE = DD ** -0.5
SLOTS = 64
NBLK = T // SLOTS
RING = 6
NGRP = -(-NE // RING)
YBUF = 3
SLOT_W = 3 * D * FF // P
MAGIC = 0x5F3759DF

CONST = {}
_at = 0
for _n, _w in (("ident", P), ("upper", P), ("cos_m", 4 * 16), ("sin_m", 4 * 16), ("cos_d", 4 * 8),
               ("sin_d", 4 * 8), ("iota_e", NE), ("rev_e", NE), ("rev_g", NG), ("steps", NBLK - 1),
               ("pack", RING), ("before_g", NGRP * NGRP), ("map_rows", 2)):
    CONST[_n] = (_at, _w)
    _at += _w
CONST_W = _at


def constants():
    c = np.zeros((P, CONST_W), np.float32)

    def put(name, value):
        a, w = CONST[name]
        c[:, a:a + w] = np.asarray(value, np.float32).reshape(-1, w)

    put("ident", np.eye(P))
    put("upper", np.triu(np.ones((P, P)), 1))
    for rot, cn, sn in ((ROPE, "cos_m", "sin_m"), (ROT, "cos_d", "sin_d")):
        half = rot // 2
        inv = np.float32(THETA) ** (-np.arange(half, dtype=np.float32) / np.float32(half))
        ang = np.arange(S_SAMPLE, dtype=np.float32)[:, None] * inv.astype(np.float32)[None, :]
        put(cn, np.cos(ang).reshape(4, P, half).transpose(1, 0, 2))
        put(sn, np.sin(ang).reshape(4, P, half).transpose(1, 0, 2))
    put("iota_e", np.arange(NE))
    put("rev_e", NE - np.arange(NE))
    put("rev_g", NG - np.arange(NG))
    put("steps", SLOTS * np.arange(1, NBLK))
    put("pack", 16.0 ** np.arange(RING))
    put("map_rows", np.arange(P)[:, None] // DD == np.arange(2)[None, :])
    g = np.arange(NGRP)
    put("before_g", g[None, :] < g[:, None])
    return c


def units():
    out = []
    for seq0, nt in ((0, 2), (2, 4)):
        for j in range(4):
            for qt in range(nt):
                out += [(seq0, nt, "mla", j, qt), (seq0, nt, "diff", j, qt)]
    return out


UNITS = units()
N_UNITS = len(UNITS)
BEFORE = [sum(1 for v in UNITS[:u] if v[2] == UNITS[u][2]) for u in range(N_UNITS)]


def is_mla(u):
    return UNITS[u][2] == "mla"


def batch(u):
    seq0, nt, kind, j, qt = UNITS[u]
    return j + (4 if seq0 else 0)


def ends_batch(u):
    return not is_mla(u) and UNITS[u][4] == UNITS[u][1] - 1


TRANSPOSES = []
O_LAG = 6
for _i in range(N_UNITS + O_LAG + 1):
    if 0 <= _i - 2 < N_UNITS:
        TRANSPOSES += [("p", _i - 2, a) for a in range(2 if is_mla(_i - 2) else 1)]
    if 0 <= _i - O_LAG < N_UNITS and ends_batch(_i - O_LAG):
        TRANSPOSES.append(("o", _i - O_LAG, 0))
TURN = {x: n for n, x in enumerate(TRANSPOSES)}


def p_transposed(u):
    return TURN[("p", u, 1 if is_mla(u) else 0)] + 1


def build(nc, A):
    f32, u32, i32, bf16 = (mybir.dt.float32, mybir.dt.uint32, mybir.dt.int32, mybir.dt.bfloat16)
    ALU = mybir.AluOpType
    ACT = mybir.ActivationFunctionType
    X_ = mybir.AxisListType.X

    h2_dram = nc.dram_tensor("h2_rows", (T, D), f32).ap()
    ids_dram = nc.dram_tensor("pair_of_slot", (T * NE, 1), u32).ap()
    x2_dram = nc.dram_tensor("residual", (T, D), f32).ap()
    y_dram = nc.dram_tensor("pair_rows", (4 * T, D // 2), f32).ap()

    with ExitStack() as ctx:
        def sem(name):
            return ctx.enter_context(nc.semaphore(name))

        WORDS = 53200
        arena = ctx.enter_context(nc.sbuf_tensor("arena", [P, WORDS], f32))
        psum = ctx.enter_context(nc.psum_tensor("banks", [P, 8, 512], f32))

        def bank(b):
            return psum[:, b, :]

        class Area:

            def __init__(self, at, end):
                self.at, self.end = at, end

            def take(self, words):
                a = self.at
                self.at += words
                assert self.at <= self.end, (self.at, self.end)
                return arena[:, a:a + words]

        X0 = 0
        W0 = X0 + NT * D
        QKV0 = W0 + 2 * DC * 512
        R0 = QKV0 + 4 * SLOT_W
        K0 = R0 + DC * T
        M0 = K0 + 1276

        x_tok = arena[:, X0:X0 + NT * D].rearrange("p (t d) -> p t d", t=NT)
        xgT = arena[:, R0:R0 + DC * T].rearrange("p (t c n) -> p t c n", t=NT, c=DC)
        aT = arena[:, R0:R0 + DC * T].rearrange("p (c n) -> p c n", c=DC)
        w_buf = [arena[:, W0 + i * 4096:W0 + (i + 1) * 4096] for i in range(2)]
        w_out_sb = arena[:, W0:W0 + 8192].rearrange("p (c n) -> p c n", c=DC)
        q = Area(QKV0, R0)
        qT = q.take(HEADS * T).rearrange("p (h n) -> p h n", h=HEADS)
        kT = q.take(HEADS * T).rearrange("p (h n) -> p h n", h=HEADS)
        v_tok = q.take(NT * 512).rearrange("p (t n) -> p t n", t=NT)
        vd_words = q.take(NT * 512)
        vd_tok = vd_words.rearrange("p (t n) -> p t n", t=NT)
        w_uq_sb = vd_words[:, 0:2 * 768].rearrange("p (c n) -> p c n", c=2)
        w_ukv_sb = vd_words[:, 1536:1536 + 1024]
        qdT = q.take(DH * T).rearrange("p (h n) -> p h n", h=DH)
        kdT = q.take(DH * T).rearrange("p (h n) -> p h n", h=DH)
        ring = [arena[:, a:a + SLOT_W] for a in [QKV0 + s * SLOT_W for s in range(4)] + [R0, W0]]

        def is_last(g, s):
            return isinstance(g, int) and g * RING + s == NE - 1

        def weights(g, s):
            return x_tok.rearrange("p t d -> p (t d)") if is_last(g, s) else ring[s]

        k = Area(K0, M0)
        const_sb = k.take(CONST_W)

        def const(name):
            a, w = CONST[name]
            return const_sb[:, a:a + w]

        ident = const("ident")
        gain_in = k.take(DC)
        gains = k.take(4)
        gain_q, gain_kv, gain_sub = gains[:, 0:2], gains[:, 2:3], gains[:, 3:4]
        pairid = k.take(2 * NT).bitcast(u32)
        slot_u = k.take(2 * NT).bitcast(u32)
        gates = k.take(2 * NT)
        yids_sb = k.take(NBLK * NE).bitcast(u32)
        neglam = k.take(1)
        ss = k.take(NT)
        rs = k.take(NT)
        ss_c = k.take(2 * NT)
        rs_c = k.take(2 * NT)
        nw = k.take(3 * 8)
        nw_pool = k.take(3 * 8)

        m = Area(M0, WORDS)
        c_tok = [m.take(LATENT) for _ in range(3)]
        qk_tok = [m.take(512) for _ in range(2)]
        q_tok = m.take(HEADS * QK)
        k_tok = m.take(HEADS * QK)
        cT = [m.take(3 * P) for _ in range(2)]
        rope_t = m.take(4 * P)
        kpe_t = m.take(4 * 16 + ROPE)
        junk = m.take(512).bitcast(bf16)
        junk_l = m.take(192).bitcast(bf16)
        lam_in = m.take(4 * DD)
        lam_t = m.take(DD)
        lam_s = m.take(4)
        m = Area(M0, WORDS)
        p_tok = [m.take(1024).rearrange("p (a n) -> p a n", a=2) for _ in range(3)]
        pT = [m.take(1024).rearrange("p (a k n) -> p a k n", a=2, k=4) for _ in range(2)]
        q_pad = [m.take(2 * P).rearrange("p (a n) -> p a n", a=2) for _ in range(2)]
        od = [m.take(512).rearrange("p (q n) -> p q n", q=4) for _ in range(2)]
        mx = m.take(8).rearrange("p (u a) -> p u a", a=2)
        nbias = m.take(8).rearrange("p (u a) -> p u a", a=2)
        l_sum = m.take(12).rearrange("p (u a) -> p u a", a=2)
        rl = m.take(12).rearrange("p (u a) -> p u a", a=2)
        cmix = m.take(2)
        so = m.take(8)
        ro = m.take(8)
        junk_o = m.take(64).bitcast(bf16)
        m = Area(M0, WORDS)
        h2 = [m.take(D) for _ in range(2)]
        h2T = m.take(D).rearrange("p (c n) -> p c n", c=DC)
        gain_ffn = m.take(D)
        m1_all = m.take(NT * NE).rearrange("p (t e) -> p t e", t=NT)
        m2_all = m.take(NT * NE).rearrange("p (t e) -> p t e", t=NT)
        m12 = m.take(NT * NE).rearrange("p (t e) -> p t e", t=NT)
        macc = m.take(NT * NE).rearrange("p (t e) -> p t e", t=NT)
        w_r = m.take(DC * (NG + NE)).rearrange("p (c n) -> p c n", c=DC)
        bias_r = m.take(NG + NE)
        ones = m.take(P)
        logit = m.take(NG + NE)
        r_small = m.take(16)
        r_g = m.take(3 * NG)
        r_e = m.take(4 * NE)
        slot_f = m.take(2)
        junk_c = m.take(512).bitcast(bf16)
        cnt = m.take(NE)
        over = m.take(NE * (NBLK - 1))
        extra = m.take(NGRP * RING)
        pk = m.take(NGRP * RING)
        packed_i = k.take(2 * NGRP).bitcast(i32)
        ids_sb = const_sb[:, CONST["upper"][0]:CONST["rev_g"][0]].bitcast(u32)[:, 0:NBLK * NE]
        m = Area(M0, WORDS)
        x_pair = [m.take(D) for _ in range(RING // 2 + 1)]
        x_rows = [x_pair[i // 2][(i % 2) * SLOTS:(i % 2 + 1) * SLOTS, :] for i in range(RING + 1)]
        x_eT = [m.take(DC * SLOTS).rearrange("p (c n) -> p c n", c=DC) for _ in range(3)]
        silu_t = [m.take(P) for _ in range(3)]
        h_tok = [m.take(P) for _ in range(3)]
        h_T = [m.take(P) for _ in range(2)]
        id_cur = m.take(RING + 1).bitcast(u32)
        yid_cur = m.take(YBUF + 1).bitcast(u32)
        m = Area(W0 + SLOT_W, QKV0)
        y_sb = [m.take(512) for _ in range(YBUF + 1)]
        m = Area(QKV0, R0)
        y_rows = m.take(2 * NT * D).rearrange("p (i d) -> p i d", i=2 * NT)
        gain_fin = m.take(D)
        junk_e = m.take(512).bitcast(bf16)
        x_fin = ring[3].rearrange("p (t d) -> p t d", t=NT)

        x_in = [sem(f"x_in{t}") for t in range(NT)]
        xT_in = [sem(f"xT_in{t}") for t in range(NT)]
        win_in = [sem(f"win_in{g}") for g in range(4)]
        win0_rest_in = sem("win0_rest_in")
        const_in = sem("const_in")
        gain_loaded = sem("gain_loaded")
        wup_in = sem("wup_in")
        lam_loaded = sem("lam_loaded")
        wout_in = sem("wout_in")
        router_in = sem("router_in")
        gffn_in = sem("gffn_in")
        dve_chain = sem("dve_chain")
        act_chain = sem("act_chain")
        pool_chain = sem("pool_chain")
        xg_ready = sem("xg_ready")
        ss_ready = sem("ss_ready")
        rs_ready = sem("rs_ready")
        proj_done = sem("proj_done")
        proj_out = sem("proj_out")
        ssc_ready = sem("ssc_ready")
        rsc_ready = sem("rsc_ready")
        cT_psum = sem("cT_psum")
        cT_ready = sem("cT_ready")
        up_done = sem("up_done")
        q_out = sem("q_out")
        kv_out = sem("kv_out")
        q_roped = sem("q_roped")
        k_roped = sem("k_roped")
        qkT_psum = sem("qkT_psum")
        qT_ready = sem("qT_ready")
        kT_ready = sem("kT_ready")
        d_roped = sem("d_roped")
        dT_psum = sem("dT_psum")
        dT_ready = sem("dT_ready")
        zero_ready = sem("zero_ready")
        ones_ready = sem("ones_ready")
        lam_e = sem("lam_e")
        lam_ready = sem("lam_ready")

        scores = sem("scores")
        nbias_ready = sem("nbias_ready")
        exps = sem("exps")
        qpad_ready = sem("qpad_ready")
        rl_ready = sem("rl_ready")
        p0_normed = sem("p0_normed")
        p1_normed = sem("p1_normed")
        p_mixed = sem("p_mixed")
        pT_psum = sem("pT_psum")
        pT_dve = sem("pT_dve")
        pT_act = sem("pT_act")
        pv_done = sem("pv_done")
        o_mla = sem("o_mla")
        o_diff = sem("o_diff")
        od_scaled = sem("od_scaled")
        odT_ready = sem("odT_ready")

        oproj = sem("oproj")
        x2_ready = sem("x2_ready")
        ss2_ready = sem("ss2_ready")
        h2_ready = sem("h2_ready")
        h2_stored = [sem(f"h2_stored{i}") for i in range(2)]
        h2T_psum = sem("h2T_psum")
        h2T_ready = sem("h2T_ready")
        logits = sem("logits")
        route_neg = sem("route_neg")
        route_exp = sem("route_exp")
        masks = sem("masks")
        ranks = sem("ranks")
        slots_ready = sem("slots_ready")
        counts_psum = sem("counts_psum")
        counts_ready = sem("counts_ready")
        ids_zeroed = sem("ids_zeroed")
        ids_scattered = sem("ids_scattered")
        ids_loaded = [sem(f"ids_loaded{h}") for h in range(2)]
        ids_ready = sem("ids_ready")
        yid_ready = sem("yid_ready")
        waited = sem("waited")
        e_yid = sem("e_yid")

        last_loaded = sem("last_loaded")
        gate_loaded = [sem(f"gate_loaded{s}") for s in range(RING)]
        up_loaded = [sem(f"up_loaded{s}") for s in range(RING)]
        down_loaded = [sem(f"down_loaded{s}") for s in range(RING)]
        id_ready = sem("id_ready")
        rows_in = [sem(f"rows_in{i}") for i in range(RING + 1)]
        xeT_psum = sem("xeT_psum")
        xeT_ready = sem("xeT_ready")
        gu_done = sem("gu_done")
        silu_done = sem("silu_done")
        h_ready = sem("h_ready")
        hT_psum = sem("hT_psum")
        hT_ready = sem("hT_ready")
        down_done = sem("down_done")
        y_out = sem("y_out")
        y_stored = [sem(f"y_stored{i}") for i in range(YBUF + 1)]
        e_id = sem("e_id")
        e_xeT_psum = sem("e_xeT_psum")
        e_xeT = sem("e_xeT")
        e_gu = sem("e_gu")
        e_silu = sem("e_silu")
        e_h = sem("e_h")
        e_hT_psum = sem("e_hT_psum")
        e_hT = sem("e_hT")
        e_down = sem("e_down")
        e_y = sem("e_y")
        all_stored = sem("all_stored")
        y1_in = sem("y1_in")
        x2_stored = sem("x2_stored")
        x_back = sem("x_back")
        yrows_in = [sem(f"yrows_in{t}") for t in range(NT)]
        y_added = sem("y_added")
        ss3_ready = sem("ss3_ready")
        rs3_ready = sem("rs3_ready")
        final_ready = sem("final_ready")
        out_stored = sem("out_stored")

        block = ctx.enter_context(nc.Block())

        win_v = A["w_in"].rearrange("(p c) n -> p c n", c=DC)

        def group_w(g):
            return w_buf[g % 2][:, 0:DC * GROUP_COLS[g]].rearrange("p (c n) -> p c n", c=DC)

        def load_counts(engine, g):
            at = [g, g + NGRP]
            return [engine.value_load(packed_i[0:1, bass.ds(i, 1)], min_val=0, max_val=(1 << 24) - 1) for i in at]

        def logit_bank(t):
            return 6 if t < NT - 1 else 0

        def extras(words, s):
            v, before = words
            n = nc.s_assert_within((v // 16 ** s) % 16, 0, NBLK - 1, skip_runtime_bounds_check_because=(
                "an expert has at most T tokens"))
            for i in range(s):
                before = before + (v // 16 ** i) % 16
            return n, before

        def members(g):
            return range(min(RING, NE - g * RING)) if isinstance(g, int) else range(RING)

        def rsqrt(engine, link, scratch, dst, src, n, scale):
            x, hx, t = (scratch[:, i * 8:i * 8 + n] for i in range(3))
            link(engine.tensor_scalar(x, src, scale, EPS, ALU.mult, ALU.add))
            link(engine.tensor_scalar(dst.bitcast(i32), x.bitcast(i32), -0.5, float(MAGIC), ALU.mult, ALU.add))
            link(engine.tensor_scalar(hx, x, -0.5, None, ALU.mult))
            for step in range(3):
                link(engine.tensor_tensor(t, dst, dst, ALU.mult))
                link(engine.tensor_tensor(t, t, hx, ALU.mult))
                if engine is nc.gpsimd:
                    link(engine.tensor_scalar(t, t, 1.5, None, ALU.add))
                    last = engine.tensor_tensor(dst, t, dst, ALU.mult)
                else:
                    last = engine.scalar_tensor_tensor(dst, t, 1.5, dst, ALU.add, ALU.mult)
                if step < 2:
                    link(last)
            return last

        @block.sync
        def _(sp):
            sp.dma_start(gain_in, A["attn_norm"].rearrange("o (p c) -> (o p) c", c=DC)).then_inc(gain_loaded, 16)
            sp.dma_start(xgT[:, 0, :, :], A["xT"][:, 0, :, :]).then_inc(xT_in[0], 16)
            for i, what in enumerate((win_in[0], win0_rest_in)):
                c = slice(i * DC // 2, (i + 1) * DC // 2)
                sp.dma_start(group_w(0)[:, c, :], win_v[:, c, 0:LATENT]).then_inc(what, 16)
            sp.dma_start(x_tok[:, 0, :], A["x"][0:P, :]).then_inc(x_in[0], 16)
            sp.dma_start(const_sb, A["consts"]).then_inc(const_in, 16)
            sp.dma_start(gains, A["gains"]).then_inc(const_in, 16)
            sp.dma_start(pairid, A["pairid"]).then_inc(const_in, 16)
            for t in range(1, NT):
                sp.dma_start(xgT[:, t, :, :], A["xT"][:, t, :, :]).then_inc(xT_in[t], 16)
                sp.dma_start(x_tok[:, t, :], A["x"][t * P:(t + 1) * P, :]).then_inc(x_in[t], 16)
                if t == 1:
                    sp.dma_start(w_uq_sb, A["w_uq"][0].rearrange("(c p) n -> p c n", p=P)).then_inc(wup_in, 16)
                    sp.dma_start(w_ukv_sb, A["w_ukv"][0]).then_inc(wup_in, 16)
                    for i, n in enumerate(("diff_lq1", "diff_lk1", "diff_lq2", "diff_lk2")):
                        sp.dma_start(lam_in[:, i * DD:(i + 1) * DD],
                                     A[n].to_broadcast([P, DD])).then_inc(lam_loaded, 16)
            for g in range(1, 4):
                if g >= 2:
                    sp.wait_ge(proj_done, 6 * (g - 2) + 6)
                sp.dma_start(group_w(g), win_v[:, :, GROUP_AT[g]:GROUP_AT[g] + 512]).then_inc(win_in[g], 16)
            sp.wait_ge(proj_done, 24)
            sp.dma_start(w_out_sb, A["w_out"][0].rearrange("(c p) n -> p c n", p=P)).then_inc(wout_in, 16)
            sp.wait_ge(zero_ready, 1)
            sp.dma_start(ids_dram.rearrange("(b r e) o -> r b (e o)", b=NBLK, e=NE),
                         yids_sb[0:SLOTS, :].rearrange("r (b e) -> r b e", b=NBLK)).then_inc(ids_zeroed, 16)
            sp.wait_ge(odT_ready, 8)
            sp.wait_ge(o_mla, N_UNITS // 2)
            sp.dma_start(gain_ffn, A["ffn_norm"].to_broadcast([P, D])).then_inc(gffn_in, 16)
            sp.dma_start(w_r[:, :, 0:NG], A["router_group"][0].rearrange("(p c) n -> p c n", c=DC)).then_inc(router_in, 16)
            sp.dma_start(w_r[:, :, NG:NG + NE], A["router_expert"][0].rearrange("(p c) n -> p c n", c=DC)).then_inc(router_in, 16)
            sp.dma_start(bias_r[:, 0:NG], A["router_group_bias"].to_broadcast([P, NG])).then_inc(router_in, 16)
            sp.dma_start(bias_r[:, NG:NG + NE], A["router_expert_bias"].to_broadcast([P, NE])).then_inc(router_in, 16)

            def load_expert(g, s):
                e = g * RING + s
                w = weights(g, s)
                last = is_last(g, s)
                later = not isinstance(g, int) or g > 0 and not last
                before = (s - 1) % RING
                turn = 16 * (g + (s - 1) // RING + 1)

                def paced(what, count):
                    if later:
                        sp.wait_ge(what, count)
                        sp.sem_inc(waited, 1)

                paced(down_done, e - RING + 1)
                for i, (n, pace) in enumerate((("w_gate", (up_loaded[before], turn)),
                                               ("w_up", (down_loaded[before], turn)))):
                    paced(*pace)
                    sp.dma_start(w[:, i * 2048:(i + 1) * 2048],
                                 A[n][0, bass.ds(e, 1), :, :].rearrange("o (p c) n -> p (o c n)", c=DC)
                                 ).then_inc(last_loaded if last else (gate_loaded, up_loaded)[i][s], 16)
                paced(gate_loaded[s], 16 * (g + 1))
                sp.dma_start(w[:, 4096:6144].rearrange("p (j n) -> p j n", j=2),
                             A["w_down"][0, bass.ds(e, 1), :, :].rearrange("o (j p) n -> p (o j) n", p=P)
                             ).then_inc(last_loaded if last else down_loaded[s], 16)

            sp.wait_ge(pv_done, N_UNITS)
            for s in range(4):
                load_expert(0, s)
            def store_residual(t):
                sp.wait_ge(x2_ready, 2 * t + 2)
                sp.dma_start(x2_dram[t * P:(t + 1) * P, :], x_tok[:, t, :]).then_inc(x2_stored, 16)

            for t in range(NT - 1):
                store_residual(t)
            sp.wait_ge(oproj, 2 * NT)
            load_expert(0, 4)
            load_expert(0, 5)
            store_residual(NT - 1)
            sp.wait_ge(ids_scattered, 2 * NT * 16)
            for h in range(2):
                sp.dma_start(yids_sb[h * SLOTS:(h + 1) * SLOTS, :].rearrange("r (b e) -> r b e", b=NBLK),
                             ids_dram.rearrange("(b r e) o -> r b (e o)", b=NBLK, e=NE)).then_inc(ids_loaded[h], 16)
            sp.wait_ge(x2_stored, NT * 16)
            sp.wait_ge(h2_ready, NT)
            sp.wait_ge(ss2_ready, NT)
            sp.wait_ge(rows_in[1], 16)
            load_expert(NGRP - 1, members(NGRP - 1)[-1])
            with sp.Fori(1, NGRP - 1) as g:
                for s in range(RING):
                    load_expert(g, s)
            for s in members(NGRP - 1)[:-1]:
                load_expert(NGRP - 1, s)
            sp.wait_ge(down_done, NE - 4)
            residual = x2_dram.rearrange("(t p) d -> t p d", p=P)
            for t in range(NT):
                sp.dma_start(x_fin[:, t, :], residual[t]).then_inc(x_back, 16)
            sp.dma_start(gain_fin, A["final_norm"].rearrange("(o n) -> o n", o=1).to_broadcast([P, D])).then_inc(x_back, 16)
            sp.wait_ge(down_done, NE)
            sp.wait_ge(all_stored, 2)
            pairs = y_dram.rearrange("(t p i) n -> t p (i n)", t=NT, i=4)
            for i, what in enumerate((yrows_in[0], y1_in)):
                sp.dma_start(y_rows[:, i, :], pairs[0][:, i * D:(i + 1) * D]).then_inc(what, 16)
            for t in range(1, NT):
                sp.dma_start(y_rows[:, 2 * t:2 * t + 2, :].rearrange("p i n -> p (i n)"), pairs[t]).then_inc(yrows_in[t], 16)
            for t in range(NT):
                sp.wait_ge(final_ready, t + 1)
                out = A["y_prompt"][0, t * P:(t + 1) * P, :] if t < 2 else A["y_sample"][0, (t - 2) * P:(t - 1) * P, :]
                if t < NT - 1:
                    sp.dma_start(out, y_rows[:, 2 * t, :]).then_inc(out_stored, 16)
            for h in range(2):
                sp.wait_ge(final_ready, NT + h)
                half = slice(h * 512, (h + 1) * 512)
                sp.dma_start(out[:, half], y_rows[:, 2 * NT - 2, half]).then_inc(out_stored, 16)
            sp.wait_ge(out_stored, (NT + 1) * 16)

        @block.gpsimd
        def _(pool):
            chain = [0]

            def link(ins):
                chain[0] += 1
                ins.then_inc(pool_chain, 1)
                pool.wait_ge(pool_chain, chain[0])

            def rotary(x1, x2, cos, sin, t, shape):
                a = [t[:, i, 0:shape[1] * shape[2]].rearrange("p (a b) -> p a b", a=shape[1]) for i in range(4)]
                c, s = cos.to_broadcast(shape), sin.to_broadcast(shape)
                pool.tensor_tensor(a[0], x1, c, ALU.mult).then_inc(pool_chain, 1)
                pool.tensor_tensor(a[1], x2, s, ALU.mult).then_inc(pool_chain, 1)
                pool.tensor_tensor(a[2], x2, c, ALU.mult).then_inc(pool_chain, 1)
                pool.tensor_tensor(a[3], x1, s, ALU.mult).then_inc(pool_chain, 1)
                chain[0] += 4
                pool.wait_ge(pool_chain, chain[0])
                link(pool.tensor_tensor(x1, a[0], a[1], ALU.subtract))
                return pool.tensor_tensor(x2, a[2], a[3], ALU.add)

            def angle(name, t, half):
                tt = t if t < 2 else t - 2
                return const(name)[:, tt * half:(tt + 1) * half].unsqueeze(1)

            pool.memset(yids_sb, 2 * T).then_inc(zero_ready, 1)
            pool.wait_ge(const_in, 3 * 16)
            rt = rope_t.rearrange("p (i n) -> p i n", i=4)
            kt = kpe_t[:, 0:64].rearrange("p (i n) -> p i n", i=4)
            kr = kpe_t[:, 64:64 + ROPE]
            q3 = q_tok.rearrange("p (h n) -> p h n", h=HEADS)
            k3 = k_tok.rearrange("p (h n) -> p h n", h=HEADS)

            def key_rotary(t):
                pool.wait_ge(proj_out, t + 1)
                x = c_tok[t % 3][:, Q_RANK + KV_RANK:LATENT].unsqueeze(1)
                last = rotary(x[:, :, 0:16], x[:, :, 16:32], angle("cos_m", t, 16), angle("sin_m", t, 16),
                              kt, [P, 1, 16])
                link(last)
                if t:
                    pool.wait_ge(qkT_psum, t)
                pool.tensor_copy(k3[:, :, NOPE:QK], x.to_broadcast([P, HEADS, ROPE])).then_inc(k_roped, 1)

            def query_rotary(t):
                pool.wait_ge(q_out, t + 1)
                last = rotary(q3[:, :, NOPE:NOPE + 16], q3[:, :, NOPE + 16:QK], angle("cos_m", t, 16),
                              angle("sin_m", t, 16), rt, [P, HEADS, 16])
                last.then_inc(q_roped, 1)
                pool.wait_ge(q_roped, t + 1)

            for i in range(25):
                mm = i - 1
                if 6 <= mm < 18:
                    d, t = mm - 6, mm % 6
                    pool.wait_ge(proj_out, mm + 1)
                    v = qk_tok[mm % 2].rearrange("p (h n) -> p h n", h=2 * DH)
                    last = rotary(v[:, :, 0:8], v[:, :, 8:16], angle("cos_d", t, 8), angle("sin_d", t, 8),
                                  rt, [P, 2 * DH, 8])
                    last.then_inc(d_roped, 1)
                    pool.wait_ge(d_roped, d + 1)
                if 2 <= i < 8:
                    key_rotary(i - 2)
                    query_rotary(i - 2)

            pool.wait_ge(dT_ready, 12)
            pool.wait_ge(qT_ready, 6)
            pool.wait_ge(lam_ready, 1)
            pool.wait_ge(proj_out, 24)
            def pad(u):
                seq0, nt, kind, j, qt = UNITS[u]
                d = BEFORE[u]
                if d >= 2:
                    pool.wait_ge(scores, 2 * (u - 4) + 2)
                tok = slice((seq0 + qt) * P, (seq0 + qt + 1) * P)
                for a in range(2):
                    pool.tensor_scalar(q_pad[d % 2][:, a, :], qdT[:, j, tok], const("map_rows")[:, a:a + 1], None,
                                       ALU.mult).then_inc(qpad_ready, 1)

            def od_norm(u):
                b, nt = batch(u), UNITS[u][1]
                pool.wait_ge(o_diff, 2 * BEFORE[u] + 2)
                r = ro[:, 4 * (b % 2):4 * (b % 2) + nt]
                link(rsqrt(pool, link, nw_pool, r, so[:, 4 * (b % 2):4 * (b % 2) + nt], nt, 1.0 / (2 * DD)))

            def od_scale(u, tiles):
                b = batch(u)
                for qt in tiles:
                    o = od[b % 2][:, qt, :]
                    r = 4 * (b % 2) + qt
                    pool.tensor_scalar(o, o, ro[:, r:r + 1], None, ALU.mult).then_inc(od_scaled, 1)

            pad(1)
            for u in range(N_UNITS):
                if u + 2 < N_UNITS and not is_mla(u + 2):
                    pad(u + 2)
                if u >= 3 and ends_batch(u - 3):
                    od_norm(u - 3)
                if u >= 4 and ends_batch(u - 4):
                    od_scale(u - 4, range(0, 2))
                if u >= 5 and ends_batch(u - 5) and UNITS[u - 5][1] == 4:
                    od_scale(u - 5, range(2, 4))
            od_norm(N_UNITS - 1)
            od_scale(N_UNITS - 1, range(4))

            def note_pairs(t):
                pool.wait_ge(slots_ready, t + 1)
                for i in range(2):
                    pool.indirect_dma_start(ids_dram, bass.IndirectOffsetOnAxis(ap=slot_u[:, 2 * t + i:2 * t + i + 1], axis=0),
                                            pairid[:, 2 * t + i:2 * t + i + 1], None).then_inc(ids_scattered, 16)

            pool.wait_ge(ids_zeroed, 16)
            for t in range(NT):
                pool.wait_ge(h2_ready, t + 1)
                pool.dma_start(h2_dram[t * P:(t + 1) * P, :], h2[t % 2]).then_inc(h2_stored[t % 2], 16)
                if t >= 2:
                    note_pairs(t - 2)
            note_pairs(NT - 2)
            note_pairs(NT - 1)
            pool.wait_ge(ids_ready, 1)
            pool.wait_ge(h2_stored[0], 3 * 16)
            pool.wait_ge(h2_stored[1], 3 * 16)
            pool.wait_ge(counts_ready, 1)

            def await_count(what, count):
                pool.wait_ge(what, count)
                pool.sem_inc(waited, 1)

            def gather(i, column, ready, count):
                pool.tensor_copy(id_cur[0:SLOTS, i:i + 1], ids_sb[0:SLOTS, bass.ds(column, 1)]).then_inc(ready, 1)
                await_count(ready, count)
                pool.indirect_dma_start(x_rows[i], None, h2_dram,
                                        bass.IndirectOffsetOnAxis(ap=id_cur[0:SLOTS, i:i + 1], axis=0)
                                        ).then_inc(rows_in[i], 16)

            def scatter(i, column, ready, count):
                pool.tensor_copy(yid_cur[:, i:i + 1], yids_sb[:, bass.ds(column, 1)]).then_inc(ready, 1)
                await_count(ready, count)
                pool.indirect_dma_start(y_dram, bass.IndirectOffsetOnAxis(ap=yid_cur[:, i:i + 1], axis=0), y_sb[i],
                                        None, bounds_check=4 * T - 1, oob_is_err=False).then_inc(y_stored[i], 16)

            def gather_main(g, s):
                e = g * RING + s
                if not isinstance(g, int) or e >= RING:
                    await_count(xeT_psum, e - RING + 1)
                gather(s % RING, e, id_ready, e + 1)

            def store_main(g, s):
                e = g * RING + s
                await_count(y_out, e + 1)
                scatter(s % YBUF, e, yid_ready, e + 1)

            EX, YX = RING, YBUF
            AHEAD, BEHIND = 2, YBUF + 1

            def store_further(words, s, e):
                n, before = extras(words, s)
                with pool.If(n > 0):
                    await_count(e_y, before + n + 1)
                    scatter(YX, n * NE + e, e_yid, before + n)

            def rows_group(g):
                words = load_counts(pool, g)
                if not isinstance(g, int) or g:
                    words_before = load_counts(pool, g - 1)
                for s in members(g):
                    e = g * RING + s
                    if not isinstance(g, int) or e >= BEHIND:
                        store_main(g, s - BEHIND)
                    n, before = extras(words, s)
                    with pool.If(n > 0):
                        await_count(e_xeT_psum, before + 1)
                        gather(EX, NE + e, e_id, before + 1)
                    if not isinstance(g, int) or e + AHEAD < NE:
                        gather_main(g, s + AHEAD)
                    if s:
                        store_further(words, s - 1, e - 1)
                    elif not isinstance(g, int) or g:
                        store_further(words_before, RING - 1, e - 1)
                    with pool.If(n > 1):
                        with pool.Fori(0, n - 1) as j:
                            c = before + j + 1
                            await_count(e_xeT_psum, c + 1)
                            more = nc.s_assert_within(j, 0, NBLK - 3, skip_runtime_bounds_check_because="j + 1 < n < NBLK")
                            gather(EX, (more + 2) * NE + e, e_id, c + 1)
                            await_count(e_y, c + 1)
                            scatter(YX, (more + 1) * NE + e, e_yid, c)
                return words

            for s in range(AHEAD):
                gather_main(0, s)
            pool.wait_ge(ids_ready, 2)
            rows_group(0)
            with pool.Fori(1, NGRP - 1) as g:
                rows_group(g)
            words = rows_group(NGRP - 1)
            store_further(words, members(NGRP - 1)[-1], NE - 1)
            for e in range(NE - BEHIND, NE):
                store_main(NGRP - 1, e - (NGRP - 1) * RING)
            for i in range(YBUF):
                pool.wait_ge(y_stored[i], len(range(i, NE, YBUF)) * 16)
            pool.sem_inc(all_stored, 1)

            for t in range(NT - 1):
                pool.wait_ge(ss3_ready, t + 1)
                rsqrt(pool, link, nw_pool, rs[:, t:t + 1], ss[:, t:t + 1], 1, 1.0 / D).then_inc(rs3_ready, 1)
                pool.wait_ge(rs3_ready, t + 1)

        @block.scalar
        def _(act):
            chain = [0]

            def link(ins):
                chain[0] += 1
                ins.then_inc(act_chain, 1)
                act.wait_ge(act_chain, chain[0])

            def square(t):
                act.wait_ge(x_in[t], 16)
                if t:
                    act.wait_ge(ss_ready, t)
                act.activation(junk, x_tok[:, t, :], ACT.Square, accum_out=ss[:, t:t + 1]).then_inc(ss_ready, 1)

            def proj_evac(mm):
                g, t = divmod(mm, 6)
                act.wait_ge(proj_done, mm + 1)
                act.wait_ge(rs_ready, t + 1)
                src = bank(mm % 2)[:, 0:GROUP_COLS[g]]
                if g == 0:
                    if t >= 3:
                        act.wait_ge(k_roped, t - 2)
                    dst = c_tok[t % 3]
                elif g < 3:
                    if mm >= 8:
                        act.wait_ge(dT_psum, mm - 7)
                    dst = qk_tok[mm % 2]
                else:
                    if t == 0:
                        act.wait_ge(up_done, 6)
                    dst = vd_tok[:, t, :]
                act.activation(dst, src, ACT.Copy, scale=rs[:, t:t + 1]).then_inc(proj_out, 1)

            def latent_square(t):
                act.wait_ge(proj_out, t + 1)
                if t:
                    act.wait_ge(ssc_ready, 2 * t)
                act.activation(junk_l[:, 0:Q_RANK], c_tok[t % 3][:, 0:Q_RANK], ACT.Square,
                               accum_out=ss_c[:, 2 * t:2 * t + 1]).then_inc(ssc_ready, 1)
                act.activation(junk_l[:, Q_RANK:Q_RANK + KV_RANK], c_tok[t % 3][:, Q_RANK:Q_RANK + KV_RANK],
                               ACT.Square, accum_out=ss_c[:, 2 * t + 1:2 * t + 2]).then_inc(ssc_ready, 1)

            def cT_evac(t):
                act.wait_ge(cT_psum, t + 1)
                if t >= 2:
                    act.wait_ge(up_done, t - 1)
                for j in range(3):
                    gain = gain_q[:, j:j + 1] if j < 2 else gain_kv
                    last = act.activation(cT[t % 2][:, j * P:(j + 1) * P], bank(2)[:, j * P:(j + 1) * P],
                                          ACT.Copy, scale=gain)
                last.then_inc(cT_ready, 1)

            def q_evac(t):
                act.wait_ge(up_done, t + 1)
                act.wait_ge(rsc_ready, t + 1)
                if t:
                    act.wait_ge(qkT_psum, t)
                both = psum[:, 3:5, :].rearrange("p b n -> p (b n)")[:, 0:HEADS * QK]
                act.activation(q_tok, both, ACT.Copy, scale=rs_c[:, 2 * t:2 * t + 1]).then_inc(q_out, 1)

            def kT_evac(t):
                act.wait_ge(qkT_psum, t + 1)
                act.activation(kT[0:QK, :, t * P:(t + 1) * P],
                               psum[0:QK, 5:7, :].rearrange("p b (h n) -> p (b h) n", n=P),
                               ACT.Copy).then_inc(kT_ready, 1)

            act.wait_ge(const_in, 3 * 16)
            square(0)
            square(1)
            for i in range(25):
                if i == 9:
                    act.wait_ge(lam_ready, 1)
                    act.activation(lam_s[:, 2:4], lam_s[:, 0:2], ACT.Exp).then_inc(lam_e, 1)
                if i + 1 < NT and i >= 1:
                    square(i + 1)
                if 3 <= i < 9:
                    kT_evac(i - 3)
                if i < 24:
                    proj_evac(i)
                if i < 6:
                    latent_square(i)
                if 2 <= i < 8:
                    q_evac(i - 2)
                if 1 <= i < 7:
                    cT_evac(i - 1)

            t_at = 0
            act.wait_ge(d_roped, 12)
            act.wait_ge(k_roped, 6)
            for i in range(N_UNITS + 4):
                if i < N_UNITS:
                    u = i
                    seq0, nt, kind, j, qt = UNITS[u]
                    act.wait_ge(nbias_ready, u + 1)
                    if u >= 3:
                        act.wait_ge(pT_psum, p_transposed(u - 3))
                    for a in range(2):
                        act.activation(p_tok[u % 3][:, a, 0:nt * P], bank(2 * (u % 2) + a)[:, 0:nt * P], ACT.Exp,
                                       bias=nbias[:, u % 4, a:a + 1], scale=MLA_SCALE if is_mla(u) else DIFF_SCALE,
                                       accum_out=l_sum[:, u % 6, a:a + 1]).then_inc(exps, 1)
                u = i - 2
                if 0 <= u < N_UNITS and is_mla(u):
                    nt = UNITS[u][1]
                    tau = TURN[("p", u, 1)]
                    act.wait_ge(pT_psum, tau + 1)
                    act.activation(pT[u % 2][:, 1, 0:nt, :],
                                   bank(4 + tau % 2)[:, 0:nt * P].rearrange("p (k n) -> p k n", n=P),
                                   ACT.Copy).then_inc(pT_act, 1)
                u = i - 1
                if 0 <= u < N_UNITS and is_mla(u):
                    act.wait_ge(rl_ready, u + 1)
                    p = p_tok[u % 3][:, 1, 0:UNITS[u][1] * P]
                    act.activation(p, p, ACT.Copy, scale=rl[:, u % 6, 1:2]).then_inc(p1_normed, 1)
                u = i - 3
                if 0 <= u < N_UNITS:
                    seq0, nt, kind, j, qt = UNITS[u]
                    act.wait_ge(pv_done, u + 1)
                    o = bank(6 + u % 2)[:, 0:P]
                    if is_mla(u):
                        act.activation(aT[:, j, (seq0 + qt) * P:(seq0 + qt + 1) * P], o, ACT.Copy).then_inc(o_mla, 1)
                    else:
                        b = batch(u)
                        if qt == 0 and b >= 2:
                            act.wait_ge(odT_ready, b - 1)
                        act.activation(od[b % 2][:, qt, :], o, ACT.Copy, scale=rl[:, u % 6, 0:1]).then_inc(o_diff, 1)
                        act.activation(junk_o, o, ACT.Square, scale=rl[:, u % 6, 0:1],
                                       accum_out=so[:, 4 * (b % 2) + qt:4 * (b % 2) + qt + 1]).then_inc(o_diff, 1)
                        act.wait_ge(o_diff, 2 * BEFORE[u] + 2)

            def ffn_square(t):
                act.wait_ge(x2_ready, 2 * t + 2)
                if t:
                    act.wait_ge(ss2_ready, t)
                act.activation(junk_c, x_tok[:, t, :], ACT.Square, accum_out=ss[:, t:t + 1]).then_inc(ss2_ready, 1)

            act.wait_ge(odT_ready, 8)
            def h2T_evac(t):
                act.wait_ge(h2T_psum, t + 1)
                if t:
                    act.wait_ge(logits, t)
                act.activation(h2T, psum[:, 4:6, :].rearrange("p b (c n) -> p (b c) n", n=P), ACT.Copy).then_inc(h2T_ready, 1)

            def route_exps(t):
                act.wait_ge(route_neg, 2 * t + 2)
                act.activation(r_g[:, 0:NG], logit[:, 0:NG], ACT.Exp, bias=r_small[:, 0:1],
                               accum_out=r_small[:, 1:2]).then_inc(act_chain, 1)
                chain[0] += 1
                act.activation(r_small[:, 3:4], r_small[:, 2:3], ACT.Exp).then_inc(route_exp, 1)

            ffn_square(0)
            for t in range(NT - 1):
                h2T_evac(t)
                ffn_square(t + 1)
                if t < NT - 2:
                    route_exps(t)
            h2T_evac(NT - 1)
            route_exps(NT - 2)
            route_exps(NT - 1)

            act.wait_ge(counts_ready, 1)

            def further(g, s, words):
                n, before = extras(words, s)
                with act.If(n > 0):
                    with act.Fori(0, n) as j:
                        c = before + j + 1
                        act.wait_ge(e_gu, c)
                        act.activation(silu_t[2], bank(7)[:, 0:P], ACT.Silu).then_inc(e_silu, 1)
                        with act.If(c > 1):
                            act.wait_ge(y_stored[YBUF], 16 * (c - 1))
                            act.sem_inc(waited, 1)
                        act.wait_ge(e_down, c)
                        act.activation(y_sb[YBUF], bank(7), ACT.Copy).then_inc(e_y, 1)

            def y_evac(g, s):
                e = g * RING + s
                act.wait_ge(down_done, e + 1)
                if not isinstance(g, int) or e >= YBUF:
                    act.wait_ge(y_stored[s % YBUF], (g * (RING // YBUF) + s // YBUF) * 16)
                act.activation(y_sb[s % YBUF], bank(4 + s % 2), ACT.Copy).then_inc(y_out, 1)

            def act_group(g):
                words = load_counts(act, g)
                for s in members(g):
                    e = g * RING + s
                    act.wait_ge(gu_done, e + 1)
                    if not isinstance(g, int) or e >= 2:
                        act.wait_ge(h_ready, e - 1)
                    act.activation(silu_t[s % 2], bank(1 + s % 2)[:, 0:P], ACT.Silu).then_inc(silu_done, 1)
                    if not isinstance(g, int) or e >= 1:
                        y_evac(g, s - 1)
                    further(g, s, words)
                return words

            act.sem_inc(e_y, 1)
            act_group(0)
            with act.Fori(1, NGRP - 1) as g:
                act_group(g)
            words = act_group(NGRP - 1)
            y_evac(NGRP - 1, NE - 1 - (NGRP - 1) * RING)
            n, before = extras(words, members(NGRP - 1)[-1])
            with act.If(before + n > 0):
                act.wait_ge(y_stored[YBUF], 16 * (before + n))
                act.sem_inc(waited, 1)
            act.sem_inc(all_stored, 1)

            for t in range(NT):
                act.wait_ge(y_added, t + 1)
                if t:
                    act.wait_ge(ss3_ready, t)
                act.activation(junk_e, x_fin[:, t, :], ACT.Square, accum_out=ss[:, t:t + 1]).then_inc(ss3_ready, 1)

        @block.vector
        def _(dve):
            chain = [0]

            def link(ins):
                chain[0] += 1
                ins.then_inc(dve_chain, 1)
                dve.wait_ge(dve_chain, chain[0])

            def gain(t):
                dve.wait_ge(xT_in[t], 16)
                dve.tensor_tensor(xgT[:, t, :, :], xgT[:, t, :, :],
                                  gain_in.unsqueeze(2).to_broadcast([P, DC, P]), ALU.mult).then_inc(xg_ready, 1)

            def kv_evac(t):
                dve.wait_ge(up_done, t + 1)
                dve.wait_ge(rsc_ready, t + 1)
                if t:
                    dve.wait_ge(qkT_psum, t)
                kv = psum[:, 5:7, :].rearrange("p b (h n) -> p (b h) n", n=P)
                dve.tensor_scalar(k_tok.rearrange("p (h n) -> p h n", h=HEADS)[:, :, 0:NOPE], kv[:, :, 0:NOPE],
                                  rs_c[:, 2 * t + 1:2 * t + 2], None, ALU.mult)
                dve.tensor_scalar(v_tok[:, t, :].rearrange("p (h n) -> p h n", h=HEADS), kv[:, :, NOPE:P],
                                  rs_c[:, 2 * t + 1:2 * t + 2], None, ALU.mult).then_inc(kv_out, 1)

            def latent_norm(t):
                dve.wait_ge(ssc_ready, 2 * t + 2)
                link(dve.tensor_scalar(ss_c[:, 2 * t:2 * t + 1], ss_c[:, 2 * t:2 * t + 1], KV_RANK / Q_RANK, None, ALU.mult))
                rsqrt(dve, link, nw, rs_c[:, 2 * t:2 * t + 2], ss_c[:, 2 * t:2 * t + 2], 2, 1.0 / KV_RANK).then_inc(rsc_ready, 1)

            def norm_x(t):
                dve.wait_ge(ss_ready, t + 1)
                rsqrt(dve, link, nw, rs[:, t:t + 1], ss[:, t:t + 1], 1, 1.0 / D).then_inc(rs_ready, 1)
                dve.wait_ge(rs_ready, t + 1)

            dve.wait_ge(gain_loaded, 16)
            gain(0)
            gain(1)
            norm_x(0)
            norm_x(1)
            for i in range(25):
                if i == 8:
                    dve.wait_ge(lam_loaded, 4 * 16)
                    for j in range(2):
                        link(dve.tensor_tensor(lam_t, lam_in[:, 2 * j * DD:(2 * j + 1) * DD],
                                               lam_in[:, (2 * j + 1) * DD:(2 * j + 2) * DD], ALU.mult))
                        link(dve.reduce_sum(lam_s[:, j:j + 1], lam_t, X_))
                    dve.sem_inc(lam_ready, 1)
                if 1 <= i < NT - 1:
                    gain(i + 1)
                    norm_x(i + 1)
                if 3 <= i < 9:
                    t = i - 3
                    dve.wait_ge(qkT_psum, t + 1)
                    dve.tensor_copy(qT[0:QK, :, t * P:(t + 1) * P],
                                    psum[0:QK, 3:5, :].rearrange("p b (h n) -> p (b h) n", n=P)).then_inc(qT_ready, 1)
                if i < 6:
                    latent_norm(i)
                    dve.wait_ge(rsc_ready, i + 1)
                if i == 12:
                    dve.wait_ge(lam_e, 1)
                    link(dve.tensor_tensor(neglam, lam_s[:, 3:4], lam_s[:, 2:3], ALU.subtract))
                    link(dve.tensor_scalar(neglam, neglam, LAMBDA_INIT, None, ALU.subtract))
                    link(dve.tensor_scalar(gain_sub, gain_sub, 1.0 - LAMBDA_INIT, None, ALU.mult))
                mm = i - 1
                if 6 <= mm < 18:
                    d, t = mm - 6, mm % 6
                    dve.wait_ge(dT_psum, d + 1)
                    dst = qdT if d < 6 else kdT
                    dve.tensor_copy(dst[:, :, t * P:(t + 1) * P],
                                    bank(7).rearrange("p (h n) -> p h n", n=P)).then_inc(dT_ready, 1)
                if 2 <= i < 8:
                    kv_evac(i - 2)

            dve.wait_ge(proj_out, 24)
            dve.wait_ge(q_roped, 6)
            dve.wait_ge(k_roped, 6)
            dve.wait_ge(d_roped, 12)
            dve.wait_ge(cT_ready, 6)
            dve.wait_ge(up_done, 6)
            for i in range(N_UNITS + O_LAG + 1):
                if i < N_UNITS:
                    u = i
                    nt = UNITS[u][1]
                    for a in range(2):
                        dve.wait_ge(scores, 2 * u + a + 1)
                        if a == 0 and u >= 4:
                            dve.wait_ge(exps, 2 * (u - 4) + 2)
                        dve.reduce_max(mx[:, u % 4, a:a + 1], bank(2 * (u % 2) + a)[:, 0:nt * P], X_).then_inc(dve_chain, 1)
                        chain[0] += 1
                    dve.wait_ge(dve_chain, chain[0])
                    dve.tensor_scalar(nbias[:, u % 4, :], mx[:, u % 4, :], -(MLA_SCALE if is_mla(u) else DIFF_SCALE),
                                      None, ALU.mult).then_inc(nbias_ready, 1)
                u = i - 1
                if 0 <= u < N_UNITS:
                    nt = UNITS[u][1]
                    dve.wait_ge(exps, 2 * u + 2)
                    if u >= 6 and is_mla(u - 6):
                        dve.wait_ge(p1_normed, BEFORE[u - 6] + 1)
                    dve.reciprocal(rl[:, u % 6, :], l_sum[:, u % 6, :]).then_inc(rl_ready, 1)
                    dve.wait_ge(rl_ready, u + 1)
                    if is_mla(u):
                        p = p_tok[u % 3][:, 0, 0:nt * P]
                        dve.tensor_scalar(p, p, rl[:, u % 6, 0:1], None, ALU.mult).then_inc(p0_normed, 1)
                    else:
                        link(dve.scalar_tensor_tensor(cmix[:, 0:1], l_sum[:, u % 6, 0:1], neglam, rl[:, u % 6, 1:2], ALU.mult, ALU.mult))
                        p = p_tok[u % 3]
                        dve.scalar_tensor_tensor(p[:, 0, 0:nt * P], p[:, 1, 0:nt * P], cmix[:, 0:1], p[:, 0, 0:nt * P],
                                                 ALU.mult, ALU.add).then_inc(p_mixed, 1)
                        dve.wait_ge(p_mixed, BEFORE[u] + 1)
                u = i - 2
                if 0 <= u < N_UNITS:
                    nt = UNITS[u][1]
                    tau = TURN[("p", u, 0)]
                    dve.wait_ge(pT_psum, tau + 1)
                    dve.tensor_copy(pT[u % 2][:, 0, 0:nt, :],
                                    bank(4 + tau % 2)[:, 0:nt * P].rearrange("p (k n) -> p k n", n=P)
                                    ).then_inc(pT_dve, 1)
                u = i - O_LAG
                if 0 <= u < N_UNITS and ends_batch(u):
                    seq0, nt, kind, j, qt = UNITS[u]
                    tau = TURN[("o", u, 0)]
                    dve.wait_ge(pT_psum, tau + 1)
                    dve.tensor_scalar(aT[:, 4 + j, seq0 * P:(seq0 + nt) * P], bank(4 + tau % 2)[:, 0:nt * P], gain_sub, None,
                                      ALU.mult).then_inc(odT_ready, 1)

            dve.wait_ge(odT_ready, 8)
            dve.wait_ge(o_mla, N_UNITS // 2)
            dve.wait_ge(pv_done, N_UNITS)
            dve.wait_ge(p1_normed, N_UNITS // 2)
            dve.memset(ones, 1.0).then_inc(ones_ready, 1)

            def residual(t):
                for h in range(2):
                    dve.wait_ge(oproj, 2 * t + h + 1)
                    x = x_tok[:, t, h * 512:(h + 1) * 512]
                    dve.tensor_tensor(x, x, bank(2 * (t % 2) + h), ALU.add).then_inc(x2_ready, 1)

            def ffn_norm(t):
                dve.wait_ge(ss2_ready, t + 1)
                link(rsqrt(dve, link, nw, rs[:, t:t + 1], ss[:, t:t + 1], 1, 1.0 / D))
                if t == 0:
                    dve.wait_ge(gffn_in, 16)
                if t >= 2:
                    dve.wait_ge(h2_stored[t % 2], 16 * (t // 2))
                    dve.wait_ge(h2T_psum, t - 1)
                dve.scalar_tensor_tensor(h2[t % 2].rearrange("n (c p) -> n c p", c=DC),
                                         x_tok[:, t, :].rearrange("n (p c) -> n c p", c=DC), rs[:, t:t + 1],
                                         gain_ffn.rearrange("n (p c) -> n c p", c=DC), ALU.mult, ALU.mult).then_inc(h2_ready, 1)

            def first_max(key, values, rev, m, top):
                link(dve.scalar_tensor_tensor(key, values, m, rev, ALU.is_equal, ALU.mult))
                link(dve.reduce_max(top, key, X_))

            def route(t):
                dve.wait_ge(logits, t + 1)
                if t == 0:
                    dve.wait_ge(router_in, 4 * 16)
                link(dve.tensor_tensor(logit, bank(logit_bank(t))[:, 0:NG + NE], bias_r, ALU.add))
                gl, el = logit[:, 0:NG], logit[:, NG:NG + NE]
                far = r_g[:, NG:2 * NG]
                ngmax, diff, gmax, max1, max2, top = (r_small[:, i:i + 1] for i in (0, 2, 4, 5, 6, 8))
                masked, key, second = r_e[:, 0:NE], r_e[:, NE:2 * NE], r_e[:, 2 * NE:3 * NE]
                link(dve.reduce_max(gmax, gl, X_))
                first_max(far, gl, const("rev_g"), gmax, top)
                link(dve.tensor_scalar(far, far, top, -1e30, ALU.is_lt, ALU.mult))
                link(dve.tensor_tensor(masked.rearrange("p (g e) -> p g e", g=NG), el.rearrange("p (g e) -> p g e", g=NG),
                                       far.unsqueeze(2).to_broadcast([P, NG, EPG]), ALU.add))
                link(dve.reduce_max(max1, masked, X_))
                first_max(key, masked, const("rev_e"), max1, top)
                link(dve.tensor_scalar(m1_all[:, t, :], key, top, None, ALU.is_equal))
                link(dve.scalar_tensor_tensor(second, m1_all[:, t, :], -3e38, masked, ALU.mult, ALU.add))
                link(dve.reduce_max(max2, second, X_))
                first_max(key, second, const("rev_e"), max2, top)
                link(dve.tensor_scalar(m2_all[:, t, :], key, top, None, ALU.is_equal))
                link(dve.tensor_tensor(m12[:, t, :], m1_all[:, t, :], m2_all[:, t, :], ALU.add))
                if t == 0:
                    link(dve.tensor_copy(macc[:, t, :], m12[:, t, :]))
                else:
                    link(dve.tensor_tensor(macc[:, t, :], macc[:, t - 1, :], m12[:, t, :], ALU.add))
                dve.sem_inc(masks, 1)
                dve.tensor_scalar(ngmax, gmax, -1.0, None, ALU.mult).then_inc(route_neg, 1)
                dve.tensor_tensor(diff, max2, max1, ALU.subtract).then_inc(route_neg, 1)

            def gate(t):
                dve.wait_ge(route_exp, t + 1)
                link(dve.tensor_scalar(r_small[:, 7:8], r_small[:, 3:4], 1.0, None, ALU.add))
                link(dve.tensor_tensor(r_small[:, 7:8], r_small[:, 7:8], r_small[:, 1:2], ALU.mult))
                link(dve.reciprocal(gates[:, 2 * t:2 * t + 1], r_small[:, 7:8]))
                link(dve.tensor_tensor(gates[:, 2 * t + 1:2 * t + 2], gates[:, 2 * t:2 * t + 1], r_small[:, 3:4], ALU.mult))

            def slots(t):
                dve.wait_ge(ranks, t + 1)
                rank = bank(7)[:, 0:NE]
                key, prod = r_e[:, NE:2 * NE], r_e[:, 3 * NE:4 * NE]
                link(dve.scalar_tensor_tensor(key, rank, float(NE), const("iota_e"), ALU.mult, ALU.add))
                for i, mask in enumerate((m1_all, m2_all)):
                    link(dve.tensor_tensor(prod, key, mask[:, t, :], ALU.mult))
                    link(dve.reduce_sum(slot_f[:, i:i + 1], prod, X_))
                dve.tensor_copy(slot_u[:, 2 * t:2 * t + 2], slot_f).then_inc(slots_ready, 1)
                dve.wait_ge(slots_ready, t + 1)

            residual(0)
            ffn_norm(0)
            for t in range(NT):
                if t + 1 < NT:
                    residual(t + 1)
                    ffn_norm(t + 1)
                route(t)
                if t:
                    slots(t - 1)
                if t + 1 < NT:
                    gate(t)
            slots(NT - 1)
            gate(NT - 1)
            dve.wait_ge(counts_psum, 1)
            link(dve.tensor_copy(cnt[0:1, :], bank(6)[0:1, 64:64 + NE]))
            link(dve.memset(extra[0:1, :], 0.0))
            ov = over[0:1, :].rearrange("o (e k) -> o e k", e=NE)
            link(dve.tensor_tensor(ov, cnt[0:1, :].unsqueeze(2).to_broadcast([1, NE, NBLK - 1]),
                                   const("steps")[0:1, :].unsqueeze(1).to_broadcast([1, NE, NBLK - 1]), ALU.is_gt))
            link(dve.reduce_sum(extra[0:1, 0:NE], ov, X_))
            by_group = extra[0:1, :].rearrange("o (g s) -> o g s", s=RING)
            pk3 = pk[0:1, :].rearrange("o (g s) -> o g s", s=RING)
            link(dve.tensor_tensor(pk3, by_group, const("pack")[0:1, :].unsqueeze(1).to_broadcast([1, NGRP, RING]), ALU.mult))
            link(dve.reduce_sum(r_e[0:1, 0:NGRP], pk3, X_))
            link(dve.reduce_sum(r_e[0:1, 16:16 + NGRP], by_group, X_))
            bg = over[0:1, 0:NGRP * NGRP].rearrange("o (g h) -> o g h", g=NGRP)
            link(dve.tensor_tensor(bg, const("before_g")[0:1, :].rearrange("o (g h) -> o g h", g=NGRP),
                                   r_e[0:1, 16:16 + NGRP].unsqueeze(1).to_broadcast([1, NGRP, NGRP]), ALU.mult))
            link(dve.reduce_sum(r_e[0:1, NGRP:2 * NGRP], bg, X_))
            link(dve.tensor_copy(packed_i[0:1, :], r_e[0:1, 0:2 * NGRP]))
            dve.sem_inc(counts_ready, 1)
            dve.wait_ge(ids_loaded[0], 16)
            rows = ids_sb[0:SLOTS, :]
            link(dve.tensor_scalar(rows, yids_sb[0:SLOTS, :], 1, None, ALU.logical_shift_right))
            link(dve.tensor_scalar(rows, rows, float(T - 1), None, ALU.min))
            dve.sem_inc(ids_ready, 1)
            dve.wait_ge(ids_loaded[1], 16)
            dve.tensor_scalar(yids_sb, yids_sb, 2.0, const("map_rows")[:, 1:2], ALU.mult, ALU.add).then_inc(ids_ready, 1)

            def dve_group(g):
                words = load_counts(dve, g)
                for s in members(g):
                    e = g * RING + s
                    n, before = extras(words, s)
                    dve.wait_ge(silu_done, e + 1)
                    dve.tensor_tensor(h_tok[s % 2], silu_t[s % 2], bank(1 + s % 2)[:, P:2 * P], ALU.mult).then_inc(h_ready, 1)
                    if not isinstance(g, int) or e + 1 < NE:
                        dve.wait_ge(xeT_psum, e + 2)
                        dve.tensor_copy(x_eT[(s + 1) % 2], bank(0).rearrange("p (c n) -> p c n", c=DC)).then_inc(xeT_ready, 1)
                    dve.wait_ge(hT_psum, e + 1)
                    if not isinstance(g, int) or e >= 1:
                        dve.wait_ge(down_done, e)
                    dve.tensor_copy(h_T[0], bank(3)[:, 0:P]).then_inc(hT_ready, 1)
                    with dve.If(n > 0):
                        with dve.Fori(0, n) as j:
                            c = before + j + 1
                            dve.wait_ge(e_xeT_psum, c + 1)
                            dve.tensor_copy(x_eT[2], bank(6).rearrange("p (c n) -> p c n", c=DC)).then_inc(e_xeT, 1)
                            dve.wait_ge(e_silu, c)
                            dve.tensor_tensor(h_tok[2], silu_t[2], bank(7)[:, P:2 * P], ALU.mult).then_inc(e_h, 1)
                            dve.wait_ge(e_hT_psum, c)
                            dve.tensor_copy(h_T[1], bank(6)[:, 0:P]).then_inc(e_hT, 1)

            dve.wait_ge(xeT_psum, 1)
            dve.tensor_copy(x_eT[0], bank(0).rearrange("p (c n) -> p c n", c=DC)).then_inc(xeT_ready, 1)
            dve_group(0)
            with dve.Fori(1, NGRP - 1) as g:
                dve_group(g)
            dve_group(NGRP - 1)

            def final(t):
                if t < NT - 1:
                    dve.wait_ge(rs3_ready, t + 1)
                else:
                    dve.wait_ge(ss3_ready, t + 1)
                    link(rsqrt(dve, link, nw, rs[:, t:t + 1], ss[:, t:t + 1], 1, 1.0 / D))
                for half in ([slice(0, D)] if t < NT - 1 else [slice(0, 512), slice(512, D)]):
                    dve.scalar_tensor_tensor(y_rows[:, 2 * t, half], x_fin[:, t, half], rs[:, t:t + 1], gain_fin[:, half],
                                             ALU.mult, ALU.mult).then_inc(final_ready, 1)

            dve.wait_ge(x_back, (NT + 1) * 16)
            for t in range(NT):
                dve.wait_ge(yrows_in[t], 16)
                x = x_fin[:, t, :]
                link(dve.scalar_tensor_tensor(x, y_rows[:, 2 * t, :], gates[:, 2 * t:2 * t + 1], x, ALU.mult, ALU.add))
                if t == 0:
                    dve.wait_ge(y1_in, 16)
                dve.scalar_tensor_tensor(x, y_rows[:, 2 * t + 1, :], gates[:, 2 * t + 1:2 * t + 2], x, ALU.mult,
                                         ALU.add).then_inc(y_added, 1)
                if t >= 2:
                    final(t - 2)
            final(NT - 2)
            final(NT - 1)

        @block.tensor
        def _(pe):
            def proj(mm, half):
                g, t = divmod(mm, 6)
                if half == 0:
                    pe.wait_ge(win_in[g], 16)
                    pe.wait_ge(xg_ready, t + 1)
                    if mm >= 2:
                        pe.wait_ge(proj_out, mm - 1)
                elif mm == 0:
                    pe.wait_ge(win0_rest_in, 16)
                w = group_w(g)
                for c in range(4 * half, 4 * half + 4):
                    last = nc.tensor.matmul(bank(mm % 2)[:, 0:GROUP_COLS[g]], xgT[:, t, c, :], w[:, c, :],
                                            start=(c == 0), stop=(c == DC - 1))
                if half == 1:
                    last.then_inc(proj_done, 1)

            def latent_transpose(t):
                pe.wait_ge(proj_out, t + 1)
                if t:
                    pe.wait_ge(cT_ready, t)
                else:
                    pe.wait_ge(const_in, 3 * 16)
                for j in range(3):
                    last = nc.tensor.transpose(bank(2)[:, j * P:(j + 1) * P], c_tok[t % 3][:, j * P:(j + 1) * P], ident)
                last.then_inc(cT_psum, 1)

            def up(t):
                pe.wait_ge(cT_ready, t + 1)
                pe.wait_ge(wup_in, 32)
                if t:
                    pe.wait_ge(qT_ready, t)
                    pe.wait_ge(kT_ready, t)
                for b, a, n in ((3, 0, 512), (4, 512, 256)):
                    for c in range(2):
                        nc.tensor.matmul(bank(b)[:, 0:n], cT[t % 2][:, c * P:(c + 1) * P], w_uq_sb[:, c, a:a + n],
                                         start=(c == 0), stop=(c == 1))
                for h in range(2):
                    last = nc.tensor.matmul(bank(5 + h), cT[t % 2][:, 2 * P:3 * P], w_ukv_sb[:, h * 512:(h + 1) * 512],
                                            start=True, stop=True)
                last.then_inc(up_done, 1)

            def head_transpose(t):
                pe.wait_ge(q_roped, t + 1)
                pe.wait_ge(kv_out, t + 1)
                pe.wait_ge(k_roped, t + 1)
                for b, src in ((3, q_tok), (5, k_tok)):
                    for h in range(HEADS):
                        last = nc.tensor.transpose(bank(b + h // 4)[0:QK, (h % 4) * P:(h % 4 + 1) * P],
                                                   src[:, h * QK:(h + 1) * QK], ident)
                last.then_inc(qkT_psum, 1)

            def diff_transpose(mm):
                d = mm - 6
                pe.wait_ge(d_roped, d + 1)
                if d:
                    pe.wait_ge(dT_ready, d)
                for h in range(DH):
                    last = nc.tensor.transpose(bank(7)[:, h * P:(h + 1) * P], qk_tok[mm % 2][:, h * P:(h + 1) * P], ident)
                last.then_inc(dT_psum, 1)

            for i in range(25):
                if i < 24:
                    proj(i, 0)
                if 3 <= i < 9:
                    head_transpose(i - 3)
                if 6 <= i - 1 < 18:
                    diff_transpose(i - 1)
                if i < 24:
                    proj(i, 1)
                if 2 <= i < 8:
                    up(i - 2)
                if 1 <= i < 7:
                    latent_transpose(i - 1)

            def score(u):
                seq0, nt, kind, j, qt = UNITS[u]
                tok = slice((seq0 + qt) * P, (seq0 + qt + 1) * P)
                keys = slice(seq0 * P, (seq0 + nt) * P)
                if u >= 2:
                    pe.wait_ge(exps, 2 * (u - 2) + 2)
                if not is_mla(u):
                    pe.wait_ge(qpad_ready, 2 * BEFORE[u] + 2)
                for a in range(2):
                    if is_mla(u):
                        l, r = qT[0:QK, 2 * j + a, tok], kT[0:QK, 2 * j + a, keys]
                    else:
                        l, r = q_pad[BEFORE[u] % 2][:, a, :], kdT[:, j, keys]
                    nc.tensor.matmul(bank(2 * (u % 2) + a)[:, 0:nt * P], l, r, start=True, stop=True).then_inc(scores, 1)

            def wait_bank_read(tau):
                if tau >= 2:
                    kind, v, a = TRANSPOSES[tau - 2]
                    if kind == "o":
                        pe.wait_ge(odT_ready, batch(v) + 1)
                    elif a:
                        pe.wait_ge(pT_act, BEFORE[v] + 1)
                    else:
                        pe.wait_ge(pT_dve, v + 1)

            def transpose_p(u):
                nt = UNITS[u][1]
                if is_mla(u):
                    pe.wait_ge(p0_normed, BEFORE[u] + 1)
                    pe.wait_ge(p1_normed, BEFORE[u] + 1)
                else:
                    pe.wait_ge(p_mixed, BEFORE[u] + 1)
                for a in range(2 if is_mla(u) else 1):
                    tau = TURN[("p", u, a)]
                    wait_bank_read(tau)
                    for kt in range(nt):
                        last = nc.tensor.transpose(bank(4 + tau % 2)[:, kt * P:(kt + 1) * P],
                                                   p_tok[u % 3][:, a, kt * P:(kt + 1) * P], ident)
                    last.then_inc(pT_psum, 1)

            def attend(u):
                seq0, nt, kind, j, qt = UNITS[u]
                pe.wait_ge(pT_dve, u + 1)
                if is_mla(u):
                    pe.wait_ge(pT_act, BEFORE[u] + 1)
                if u >= 2:
                    if is_mla(u):
                        pe.wait_ge(o_mla, BEFORE[u - 2] + 1)
                    else:
                        pe.wait_ge(o_diff, 2 * BEFORE[u - 2] + 2)
                o = bank(6 + u % 2)[:, 0:P]
                for kt in range(nt):
                    st = dict(start=(kt == 0), stop=(kt == nt - 1))
                    if is_mla(u):
                        for a in range(2):
                            last = nc.tensor.matmul(o[a * VD:(a + 1) * VD, :],
                                                    v_tok[:, seq0 + kt, (2 * j + a) * VD:(2 * j + a + 1) * VD],
                                                    pT[u % 2][:, a, kt, :], **st)
                    else:
                        last = nc.tensor.matmul(o, pT[u % 2][:, 0, kt, :], vd_tok[:, seq0 + kt, j * P:(j + 1) * P], **st)
                last.then_inc(pv_done, 1)

            def transpose_o(u):
                b, nt = batch(u), UNITS[u][1]
                pe.wait_ge(od_scaled, 2 * (b + 1) if b < 4 else 8 + 4 * (b - 3))
                tau = TURN[("o", u, 0)]
                wait_bank_read(tau)
                for qt in range(nt):
                    last = nc.tensor.transpose(bank(4 + tau % 2)[:, qt * P:(qt + 1) * P], od[b % 2][:, qt, :], ident)
                last.then_inc(pT_psum, 1)

            def out_half(t, h):
                if t == 0 and h == 0:
                    pe.wait_ge(wout_in, 16)
                    pe.wait_ge(odT_ready, 4)
                    pe.wait_ge(o_mla, len([u for u in range(N_UNITS) if is_mla(u) and UNITS[u][0] == 0]))
                    pe.wait_ge(exps, 2 * N_UNITS)
                if t == 2 and h == 0:
                    pe.wait_ge(odT_ready, 8)
                    pe.wait_ge(o_mla, N_UNITS // 2)
                if t >= 2:
                    pe.wait_ge(x2_ready, 2 * (t - 2) + h + 1)
                for c in range(DC):
                    last = nc.tensor.matmul(bank(2 * (t % 2) + h), aT[:, c, t * P:(t + 1) * P],
                                            w_out_sb[:, c, h * 512:(h + 1) * 512], start=(c == 0), stop=(c == DC - 1))
                last.then_inc(oproj, 1)

            pe.wait_ge(qT_ready, 6)
            pe.wait_ge(kT_ready, 6)
            pe.wait_ge(dT_ready, 12)
            pe.wait_ge(proj_out, 24)
            for i in range(N_UNITS + O_LAG + 1):
                if i < N_UNITS:
                    score(i)
                if 0 <= i - 2 < N_UNITS:
                    transpose_p(i - 2)
                if 0 <= i - 3 < N_UNITS:
                    attend(i - 3)
                u = i - O_LAG
                if 0 <= u < N_UNITS and ends_batch(u):
                    transpose_o(u)
                if i in (N_UNITS + 1, N_UNITS + 3):
                    out_half(0, (i - N_UNITS) // 2)

            def h2_transpose(t):
                pe.wait_ge(h2_ready, t + 1)
                if t:
                    pe.wait_ge(h2T_ready, t)
                for c in range(DC):
                    last = nc.tensor.transpose(bank(4 + c // 4)[:, (c % 4) * P:(c % 4 + 1) * P],
                                               h2[t % 2][:, c * P:(c + 1) * P], ident)
                last.then_inc(h2T_psum, 1)

            def router(t):
                pe.wait_ge(h2T_ready, t + 1)
                if t == 0:
                    pe.wait_ge(router_in, 4 * 16)
                else:
                    pe.wait_ge(masks, min(t, NT - 2))
                for c in range(DC):
                    last = nc.tensor.matmul(bank(logit_bank(t))[:, 0:NG + NE], h2T[:, c, :], w_r[:, c, :],
                                            start=(c == 0), stop=(c == DC - 1))
                last.then_inc(logits, 1)

            def rank(t):
                pe.wait_ge(masks, t + 1)
                if t:
                    pe.wait_ge(slots_ready, t)
                out = bank(7)[:, 0:NE]
                last = nc.tensor.matmul(out, const("upper"), m12[:, t, :], start=True, stop=(t == 0))
                if t:
                    last = nc.tensor.matmul(out, ones, macc[:, t - 1, :], start=False, stop=True)
                last.then_inc(ranks, 1)

            pe.wait_ge(ones_ready, 1)
            for t in range(1, NT + 1):
                if t < NT:
                    out_half(t, 0)
                if t >= 1:
                    h2_transpose(t - 1)
                if t < NT:
                    out_half(t, 1)
                if t >= 1:
                    router(t - 1)
                if t >= 2:
                    rank(t - 2)
            rank(NT - 1)
            nc.tensor.matmul(bank(6)[:, 64:64 + NE], ones, macc[:, NT - 1, :], start=True, stop=True).then_inc(counts_psum, 1)

            def rows_transpose(b, i, chunks):
                for c in chunks:
                    half = slice((i % 2) * SLOTS, (i % 2 + 1) * SLOTS)
                    last = nc.tensor.transpose(bank(b)[:, c * SLOTS:(c + 1) * SLOTS],
                                               x_rows[i][:, c * P:(c + 1) * P], ident[half, half])
                return last

            def gate_up(b, i, w):
                w = w[:, 0:4096].rearrange("p (g c n) -> p g c n", g=2, c=DC)
                for c in range(DC):
                    for h in range(2):
                        last = nc.tensor.matmul(bank(b)[h * SLOTS:(h + 1) * SLOTS, 0:2 * P].rearrange("p (g n) -> p g n", g=2),
                                                x_eT[i][:, c, :], w[:, :, c, h * P:(h + 1) * P],
                                                start=(c == 0), stop=(c == DC - 1))
                return last

            def down(b, hT, w):
                w = w[:, 4096:6144].rearrange("p (j n) -> p j n", j=2)
                for j in range(2):
                    for h in range(2):
                        last = nc.tensor.matmul(bank(b)[h * SLOTS:(h + 1) * SLOTS, :], hT[:, j * SLOTS:(j + 1) * SLOTS],
                                                w[:, j, h * 512:(h + 1) * 512], start=(j == 0), stop=(j == 1))
                return last

            def await_count(what, count):
                pe.wait_ge(what, count)
                pe.sem_inc(waited, 1)

            def pe_group(g):
                words = load_counts(pe, g)
                for s in members(g):
                    e = g * RING + s
                    if is_last(g, s):
                        pe.wait_ge(last_loaded, 48)
                    else:
                        pe.wait_ge(gate_loaded[s], 16 * (g + 1))
                        pe.wait_ge(up_loaded[s], 16 * (g + 1))
                    first = isinstance(g, int) and e == 0
                    pe.wait_ge(xeT_ready, e + 1)
                    gate_up(1 + s % 2, s % 2, weights(g, s)).then_inc(gu_done, 1)
                    if not isinstance(g, int) or e + 1 < NE:
                        await_count(rows_in[(s + 1) % RING], 16 * (g + (s + 1) // RING + 1))
                        rows_transpose(0, (s + 1) % RING, range(DC)).then_inc(xeT_psum, 1)
                    if not first:
                        down_main(g, s - 1)
                    pe.wait_ge(h_ready, e + 1)
                    nc.tensor.transpose(bank(3)[:, 0:P], h_tok[s % 2], ident).then_inc(hT_psum, 1)
                    n, before = extras(words, s)
                    with pe.If(n > 0):
                        with pe.Fori(0, n) as j:
                            c = before + j + 1
                            await_count(rows_in[RING], 16 * c)
                            rows_transpose(6, RING, range(DC)).then_inc(e_xeT_psum, 1)
                            pe.wait_ge(e_xeT, c)
                            pe.wait_ge(e_y, c)
                            gate_up(7, 2, weights(g, s)).then_inc(e_gu, 1)
                            pe.wait_ge(e_h, c)
                            nc.tensor.transpose(bank(6)[:, 0:P], h_tok[2], ident).then_inc(e_hT_psum, 1)
                            if not is_last(g, s):
                                await_count(down_loaded[s], 16 * (g + 1))
                            pe.wait_ge(e_hT, c)
                            down(7, h_T[1], weights(g, s)).then_inc(e_down, 1)

            def down_main(g, s):
                e = g * RING + s
                if not is_last(g, s):
                    await_count(down_loaded[s % RING], 16 * (g + s // RING + 1))
                pe.wait_ge(hT_ready, e + 1)
                if not isinstance(g, int) or e >= 2:
                    pe.wait_ge(y_out, e - 1)
                down(4 + s % 2, h_T[0], weights(g, s % RING)).then_inc(down_done, 1)

            pe.sem_inc(e_xeT_psum, 1)
            pe.wait_ge(rows_in[0], 16)
            pe.wait_ge(counts_ready, 1)
            rows_transpose(0, 0, range(DC)).then_inc(xeT_psum, 1)
            pe_group(0)
            with pe.Fori(1, NGRP - 1) as g:
                pe_group(g)
            pe_group(NGRP - 1)
            down_main(NGRP - 1, NE - 1 - (NGRP - 1) * RING)


WEIGHTS = ["attn_norm", "w_in", "w_uq", "w_ukv", "diff_lq1", "diff_lk1", "diff_lq2",
           "diff_lk2", "w_out", "ffn_norm", "router_group", "router_group_bias", "router_expert",
           "router_expert_bias", "w_gate", "w_up", "w_down", "final_norm"]


def kernel(**inputs):
    import concourse.bacc as _bacc
    from concourse.bass_utils import run_bass_kernel_spmd as _run

    nc = _bacc.Bacc("TRN2", target_bir_lowering=False, num_devices=1)
    x = np.concatenate([np.asarray(inputs["x_prompt"])[0], np.asarray(inputs["x_sample"])[0]], axis=0)
    arrays = {
        "x": np.ascontiguousarray(x),
        "xT": np.ascontiguousarray(x.reshape(NT, P, P, DC).transpose(2, 0, 3, 1)),
        "consts": constants(),
        "pairid": np.ascontiguousarray(np.arange(2 * T, dtype=np.uint32).reshape(NT, P, 2).transpose(1, 0, 2).reshape(P, 2 * NT)),
    }
    arrays["gains"] = np.ascontiguousarray(np.concatenate(
        [np.asarray(inputs[n]).reshape(-1, P) for n in ("q_norm", "kv_norm", "diff_subln")], axis=0).T)
    for n in WEIGHTS:
        arrays[n] = np.ascontiguousarray(np.asarray(inputs[n]))
    arrays["w_in"] = arrays["w_in"].reshape(D, -1)
    A = {n: nc.dram_tensor(n, a.shape, mybir.dt.from_np(a.dtype), kind="ExternalInput").ap() for n, a in arrays.items()}
    for n, s in (("y_prompt", S_PROMPT), ("y_sample", S_SAMPLE)):
        A[n] = nc.dram_tensor(n, (1, s, D), mybir.dt.float32, kind="ExternalOutput").ap()
    build(nc, A)
    r = _run(nc, [arrays], core_ids=[0])
    return r.results[0]["y_prompt"], r.results[0]["y_sample"]
```
